# Optimizing a Trainium2 kernel written in Bass

```python
import math
import jax, jax.numpy as jnp
from jax import lax
import numpy as np

D_MODEL = 1024
BATCH = 1
SEQ = 512
DEPTH = 1

HEAD_DIM = 64
FOX_HEADS = 8
SB_HEADS = 8
FOX_WIDTH = FOX_HEADS * HEAD_DIM
SB_WIDTH = SB_HEADS * HEAD_DIM
MIX_WIDTH = FOX_WIDTH + SB_WIDTH
IN_COLS = 3 * FOX_WIDTH + FOX_HEADS + 3 * SB_WIDTH
Q_BLOCK = 128
FORGET_BIAS_INIT = 3.0
N_EXPERTS = 32
TOP_K = 4
D_FF = D_MODEL
SWIGLU_LIMIT = 7.0
SWIGLU_ALPHA = 1.702
EXPERT_BLOCK = 128
NORM_EPS = 1e-5

kernel_name = "hybrid_fox_stickbreak_moe_layer"

def rmsnorm(x, g):
    xf = x.astype(jnp.float32)
    y = xf * lax.rsqrt(jnp.mean(xf * xf, axis=-1, keepdims=True) + NORM_EPS)
    return (y * g.astype(jnp.float32)).astype(x.dtype)

def to_query_blocks(t):
    b, s, h, d = t.shape
    return t.reshape(b, s // Q_BLOCK, Q_BLOCK, h, d).transpose(1, 0, 2, 3, 4)

def from_query_blocks(t):
    nb, b, qb, h, d = t.shape
    return t.transpose(1, 0, 2, 3, 4).reshape(b, nb * qb, h * d)

def forgetting_attention(q, k, v, log_f):
    b, s, h, d = q.shape
    scale = 1.0 / math.sqrt(d)
    c = jnp.cumsum(log_f.astype(jnp.float32), axis=1).transpose(0, 2, 1)
    nb = s // Q_BLOCK
    c_q = c.reshape(b, h, nb, Q_BLOCK).transpose(2, 0, 1, 3)
    kpos = jnp.arange(s)

    def block(args):
        qb, cqb, i = args
        logits = jnp.einsum('bqhd,bkhd->bhqk', qb, k).astype(jnp.float32) * scale
        logits = logits + cqb[..., None] - c[:, :, None, :]
        qpos = i * Q_BLOCK + jnp.arange(Q_BLOCK)
        causal = kpos[None, :] <= qpos[:, None]
        logits = jnp.where(causal, logits, -jnp.inf)
        p = jax.nn.softmax(logits, axis=-1).astype(v.dtype)
        return jnp.einsum('bhqk,bkhd->bqhd', p, v)

    out = lax.map(block, (to_query_blocks(q), c_q, jnp.arange(nb)))
    return from_query_blocks(out)

def stick_breaking_attention(q, k, v):
    b, s, h, d = q.shape
    scale = 1.0 / math.sqrt(d)
    nb = s // Q_BLOCK
    kpos = jnp.arange(s)

    def block(args):
        qb, i = args
        z = jnp.einsum('bqhd,bkhd->bhqk', qb, k).astype(jnp.float32) * scale
        qpos = i * Q_BLOCK + jnp.arange(Q_BLOCK)
        strict = kpos[None, :] < qpos[:, None]
        log_beta = jax.nn.log_sigmoid(z)
        log_1m = jnp.where(strict, jax.nn.log_sigmoid(-z), 0.0)
        suffix = lax.cumsum(log_1m, axis=3, reverse=True) - log_1m
        a = jnp.where(strict, jnp.exp(log_beta + suffix), 0.0).astype(v.dtype)
        return jnp.einsum('bhqk,bkhd->bqhd', a, v)

    out = lax.map(block, (to_query_blocks(q), jnp.arange(nb)))
    return from_query_blocks(out)

def moe_ffn(h, w_router, b_router, w_gate_up, b_gate_up, w_down, b_down):
    t, d = h.shape
    n_assign = t * TOP_K
    logits = (h @ w_router).astype(jnp.float32) + b_router.astype(jnp.float32)
    top_vals, top_idx = lax.top_k(logits, TOP_K)
    gates = jax.nn.softmax(top_vals, axis=-1).astype(h.dtype)

    flat_e = top_idx.reshape(-1)
    flat_tok = jnp.arange(n_assign, dtype=jnp.int32) // TOP_K
    flat_w = gates.reshape(-1)
    order = jnp.argsort(flat_e)
    sorted_e = flat_e[order]
    sorted_tok = flat_tok[order]
    sorted_w = flat_w[order]

    counts = jnp.bincount(flat_e, length=N_EXPERTS)
    starts = jnp.cumsum(counts) - counts
    padded_counts = (counts + EXPERT_BLOCK - 1) // EXPERT_BLOCK * EXPERT_BLOCK
    padded_ends = jnp.cumsum(padded_counts)
    padded_starts = padded_ends - padded_counts
    rank = jnp.arange(n_assign) - starts[sorted_e]
    dest = padded_starts[sorted_e] + rank

    n_pad = (n_assign + N_EXPERTS * (EXPERT_BLOCK - 1) + EXPERT_BLOCK - 1) // EXPERT_BLOCK * EXPERT_BLOCK
    n_blocks = n_pad // EXPERT_BLOCK
    row_tok = jnp.full((n_pad,), t, dtype=jnp.int32).at[dest].set(sorted_tok)
    row_w = jnp.zeros((n_pad,), h.dtype).at[dest].set(sorted_w)
    block_start = jnp.arange(n_blocks) * EXPERT_BLOCK
    block_e = jnp.minimum(jnp.searchsorted(padded_ends, block_start, side='right'), N_EXPERTS - 1)

    h_pad = jnp.concatenate([h, jnp.zeros((1, d), h.dtype)], axis=0)
    xs = h_pad[row_tok].reshape(n_blocks, EXPERT_BLOCK, d)

    def expert_block(args):
        xb, e = args
        gu = xb @ w_gate_up[e] + b_gate_up[e]
        gate = jnp.minimum(gu[:, 0::2], SWIGLU_LIMIT)
        up = jnp.clip(gu[:, 1::2], -SWIGLU_LIMIT, SWIGLU_LIMIT)
        act = gate * jax.nn.sigmoid(SWIGLU_ALPHA * gate) * (up + 1.0)
        return act @ w_down[e] + b_down[e]

    ys = lax.map(expert_block, (xs, block_e)).reshape(n_pad, d)
    out = jax.ops.segment_sum(ys * row_w[:, None], row_tok, num_segments=t + 1)
    return out[:t]

def setup_inputs(seed: int = 0) -> dict:
    key = jax.random.key(seed)
    ks = jax.random.split(key, 16)
    f32 = jnp.float32
    nrm = lambda k, shp, s: jax.random.normal(k, shp, f32) * s
    return {
        "x": nrm(ks[0], (BATCH, SEQ, D_MODEL), 1.0),
        "attn_norm_g": 1.0 + nrm(ks[1], (D_MODEL,), 0.02),
        "w_in": nrm(ks[2], (D_MODEL, IN_COLS), D_MODEL ** -0.5),
        "b_forget": FORGET_BIAS_INIT + nrm(ks[3], (FOX_HEADS,), 0.1),
        "fox_out_g": 1.0 + nrm(ks[4], (FOX_WIDTH,), 0.02),
        "sb_out_g": 1.0 + nrm(ks[5], (SB_WIDTH,), 0.02),
        "w_out": nrm(ks[6], (MIX_WIDTH, D_MODEL), MIX_WIDTH ** -0.5),
        "ffn_norm_g": 1.0 + nrm(ks[7], (D_MODEL,), 0.02),
        "w_router": nrm(ks[8], (D_MODEL, N_EXPERTS), D_MODEL ** -0.5),
        "b_router": nrm(ks[9], (N_EXPERTS,), 0.01),
        "w_gate_up": nrm(ks[10], (N_EXPERTS, D_MODEL, 2 * D_FF), D_MODEL ** -0.5),
        "b_gate_up": nrm(ks[11], (N_EXPERTS, 2 * D_FF), 0.01),
        "w_down": nrm(ks[12], (N_EXPERTS, D_FF, D_MODEL), D_FF ** -0.5),
        "b_down": nrm(ks[13], (N_EXPERTS, D_MODEL), 0.01),
        "final_norm_g": 1.0 + nrm(ks[14], (D_MODEL,), 0.02),
    }

def reference(x, attn_norm_g, w_in, b_forget, fox_out_g, sb_out_g, w_out, ffn_norm_g,
              w_router, b_router, w_gate_up, b_gate_up, w_down, b_down, final_norm_g):
    b, s, d = x.shape
    for _ in range(DEPTH):
        h = rmsnorm(x, attn_norm_g)
        proj = h @ w_in
        o = 0
        q_a = proj[..., o:o + FOX_WIDTH].reshape(b, s, FOX_HEADS, HEAD_DIM); o += FOX_WIDTH
        k_a = proj[..., o:o + FOX_WIDTH].reshape(b, s, FOX_HEADS, HEAD_DIM); o += FOX_WIDTH
        v_a = proj[..., o:o + FOX_WIDTH].reshape(b, s, FOX_HEADS, HEAD_DIM); o += FOX_WIDTH
        f_logit = proj[..., o:o + FOX_HEADS]; o += FOX_HEADS
        q_b = proj[..., o:o + SB_WIDTH].reshape(b, s, SB_HEADS, HEAD_DIM); o += SB_WIDTH
        k_b = proj[..., o:o + SB_WIDTH].reshape(b, s, SB_HEADS, HEAD_DIM); o += SB_WIDTH
        v_b = proj[..., o:o + SB_WIDTH].reshape(b, s, SB_HEADS, HEAD_DIM)

        log_f = jax.nn.log_sigmoid((f_logit + b_forget).astype(jnp.float32))
        y_a = rmsnorm(forgetting_attention(q_a, k_a, v_a, log_f), fox_out_g)
        y_b = rmsnorm(stick_breaking_attention(q_b, k_b, v_b), sb_out_g)
        x = x + jnp.concatenate([y_a, y_b], axis=-1) @ w_out

        h2 = rmsnorm(x, ffn_norm_g).reshape(b * s, d)
        x = x + moe_ffn(h2, w_router, b_router, w_gate_up, b_gate_up, w_down, b_down).reshape(b, s, d)
    return rmsnorm(x, final_norm_g)


_drawn_inputs = setup_inputs


def setup_inputs(seed=0):
    import zlib

    import numpy as np

    out = dict(_drawn_inputs(seed))
    spreads = {}
    factors = {'b_gate_up': 8.0, 'b_down': 8.0, 'final_norm_g': 2.881}
    for name, (base, spread) in spreads.items():
        noise = np.random.default_rng([zlib.crc32(name.encode()), seed]).standard_normal(out[name].shape)
        drawn = base * np.exp(spread * noise) if base else spread * noise
        out[name] = __import__('jax').numpy.asarray(drawn.astype(out[name].dtype))
    for name, factor in factors.items():
        out[name] = (out[name] * factor).astype(out[name].dtype)
    return out
```

```python
from contextlib import ExitStack

import concourse.bass as bass
from concourse import mybir

P = 128
D = 1024
SEQ = 512
NT = SEQ // P
KD = D // P
HEADS = 8
DH = 64
GW = HEADS * DH
NE = 32
TOPK = 4
FF = 1024
BLK = 104
LIMIT = 7.0
ALPHA = 1.702
EPS = 1e-5
SCALE = 1.0 / DH ** 0.5

PIECE = 4096
SLOTS = 6
MIX_SLOTS = 4
MIX_PIECES = 8
EXTRA_MAX = SEQ * TOPK // BLK
MAXBLK = -(-SEQ // BLK)
NX = EXTRA_MAX + 2
NI = NE + NX
FAR = 4096.0
NEG = -1e30

ALU = mybir.AluOpType
ACT = mybir.ActivationFunctionType
AX = mybir.AxisListType
F32 = mybir.dt.float32
BF16 = mybir.dt.bfloat16
I32 = mybir.dt.int32
U32 = mybir.dt.uint32


def hybrid_layer(nc, x, attn_norm_g, w_in, b_forget, fox_out_g, sb_out_g, w_out, ffn_norm_g,
                 w_router, b_router, w_gate_up, b_gate_up, w_down, b_down, final_norm_g, out):
    ctx = ExitStack()
    with ctx:
        def sb(name, shape, dt=F32):
            return ctx.enter_context(nc.sbuf_tensor(name, shape, dt))

        def sem(name):
            return ctx.enter_context(nc.semaphore(name))

        h2_rows = nc.dram_tensor("h2_rows", [SEQ + P, D], F32, kind="Internal").ap()
        acc_rows = nc.dram_tensor("acc_rows", [SEQ + P, D], F32, kind="Internal").ap()
        negc_rows = nc.dram_tensor("negc_rows", [HEADS, SEQ], F32, kind="Internal").ap()

        ring = sb("ring", [P, SLOTS, PIECE])
        xres = sb("xres", [P, NT, D])
        rows = sb("rows", [P, NT, D])
        colsT = sb("colsT", [P, KD, SEQ])
        big = sb("big", [P, 12288])

        def part(base, *dims):
            n = 1
            for d in dims:
                n *= d
            v = base
            if len(dims) == 2:
                return v.rearrange("p (a b) -> p a b", b=dims[1])
            if len(dims) == 3:
                return v.rearrange("p (a b c) -> p a b c", b=dims[1], c=dims[2])
            return v

        qk = part(big[:, 0:8192], 16, SEQ)
        v_sb = part(big[:, 8192:12288], NT, 2 * GW)
        bgu_rows = big[0:NE, 8192:8192 + 2 * FF]
        negc = part(ring[:, 4, :], HEADS, SEQ)
        wk = part(ring[:, 5, :], 8, SEQ)
        zrow = ring[:, 5, 0:D]
        negtri = ring[:, 5, D:D + SEQ]

        h2T = part(big[:, 0:4096], KD, SEQ)
        onehot = part(big[:, 4096:4608], NT, TOPK, NE)
        onehot_g = part(big[:, 4608:5120], NT, TOPK, NE)
        gT = big[0:NE, 5120:5632]
        bdown_sb = big[0:NE, 5632:6656]
        itemcmp = part(big[:, 6656:6656 + NX * NE], NX, NE)
        itemcmp2 = part(big[:, 7424:7424 + NX * NE], NX, NE)
        xg = big[0:BLK, 8192:9216]
        xgT = part(big[:, 9216:9216 + KD * BLK], KD, BLK)
        actT = part(big[:, 10240:10240 + KD * BLK], KD, BLK)
        ysb = big[0:BLK, 11264:12288]
        gtile = [part(big[:, 256 * j:256 * j + 2 * BLK], 2, BLK) for j in range(2)]
        utile = [part(big[:, 512 + 256 * j:512 + 256 * j + 2 * BLK], 2, BLK) for j in range(2)]
        stile = [part(big[:, 1024 + 256 * j:1024 + 256 * j + 2 * BLK], 2, BLK) for j in range(2)]
        fing = big[:, 4096:4096 + D]

        ident = sb("ident", [P, P])
        identb = sb("identb", [P, P], BF16)
        mask_causal = sb("mask_causal", [P, P], BF16)
        mask_strict = sb("mask_strict", [P, P], BF16)
        before = sb("before", [P, P], BF16)
        ones = sb("ones", [P, P], BF16)
        g_attn = sb("g_attn", [P, KD])
        g_mix = sb("g_mix", [P, KD])
        g_ffn = sb("g_ffn", [P, KD])
        w_f = sb("w_f", [P, KD, HEADS])
        bf_b = sb("bf_b", [P, HEADS])
        w_r = sb("w_r", [P, KD, NE])
        br_b = sb("br_b", [P, NE])
        bgu = sb("bgu", [P, NE, 16])
        ssq = sb("ssq", [P, 16])
        rstd = sb("rstd", [P, 16])
        msq = sb("msq", [P, 16])
        zf = sb("zf", [P, NT, HEADS])
        lf = sb("lf", [P, NT, HEADS])
        negc_sb = sb("negc_sb", [HEADS, SEQ])
        nmax = sb("nmax", [P, 32])
        rsum = sb("rsum", [P, 32])
        rinv = sb("rinv", [P, 32])
        logits = sb("logits", [P, NT, NE])
        top8 = sb("top8", [P, NT, 8])
        topi = sb("topi", [P, NT, 8], U32)
        topf = sb("topf", [P, NT, 8])
        gexp = sb("gexp", [P, NT, TOPK])
        gsum = sb("gsum", [P, NT])
        ginv = sb("ginv", [P, NT])
        maskf = sb("maskf", [P, NT, NE])
        maskb = sb("maskb", [P, NT, NE], BF16)
        gate_et = sb("gate_et", [P, NE * NT])
        rank_et = sb("rank_et", [P, NE * NT])
        counts = sb("counts", [P, NE])
        extra = sb("extra", [P, NE])
        onesrow = sb("onesrow", [P, NE])
        cumx = sb("cumx", [P, NE])
        iota = sb("iota", [P, P])
        padrow = sb("padrow", [P, 1])
        item_e = sb("item_e", [1, NI], I32)
        item_f = sb("item_f", [P, NI])
        item_b = sb("item_b", [P, NI])
        n_items_sb = sb("n_items_sb", [1, 1], I32)
        cxj = sb("cxj", [P, NX])
        rel = sb("rel", [P, NT])
        info = sb("info", [P, NT, 4])
        sel = sb("sel", [P, NT, BLK])
        biasc = sb("biasc", [P, 16])
        pausing = sb("pausing", [1, 2])
        padsel = sb("padsel", [BLK, 1])
        idx_next = sb("idx_next", [BLK, 1], I32)
        idx_now = sb("idx_now", [BLK, 1], I32)
        gate_next = sb("gate_next", [BLK, 1])
        gate_now = sb("gate_now", [BLK, 1])

        bank = [ctx.enter_context(nc.psum_tensor(f"bank{i}", [P, 512], F32)) for i in range(8)]
        sc_bank, pt_bank, pv_bank, pj_bank = bank[0:2], bank[2:4], bank[4:6], bank[6:8]

        landed = [sem(f"landed{s}") for s in range(SLOTS)]
        x_in = [sem(f"x_in{t}") for t in range(NT)]
        g_in = sem("g_in")
        f_in = sem("f_in")
        bgu_in = sem("bgu_in")
        r_in = sem("r_in")
        bdown_in = sem("bdown_in")
        fing_in = sem("fing_in")
        pads_out = sem("pads_out")
        negc_out = sem("negc_out")
        negc_in = sem("negc_in")
        h2_out = sem("h2_out")
        acc_out = sem("acc_out")
        consts = sem("consts")
        zero_ok = sem("zero_ok")
        dstep = sem("dstep")
        astep = sem("astep")
        pstep = sem("pstep")
        xn_ready = sem("xn_ready")
        ssx = sem("ssx")
        tr_done = sem("tr_done")
        tr_used_a = sem("tr_used_a")
        tr_used_v = sem("tr_used_v")
        bgu_done = sem("bgu_done")
        bgu_read = sem("bgu_read")
        f_done = sem("f_done")
        zf_ready = sem("zf_ready")
        lf_abs = sem("lf_abs")
        lf_ready = sem("lf_ready")
        cum_done = sem("cum_done")
        negc_ready = sem("negc_ready")
        proj_done = sem("proj_done")
        proj_read = sem("proj_read")
        score_done = sem("score_done")
        softln = sem("softln")
        arg_ready = sem("arg_ready")
        prob_ready = sem("prob_ready")
        probT_done = sem("probT_done")
        probT_v = sem("probT_v")
        probT_a = sem("probT_a")
        pv_done = sem("pv_done")
        y_ready = sem("y_ready")
        ssy = sem("ssy")
        yn_ready = sem("yn_ready")
        yt_done = sem("yt_done")
        yt_read = sem("yt_read")
        op_done = sem("op_done")
        x1_ready = sem("x1_ready")
        ss1 = sem("ss1")
        h2_ready = sem("h2_ready")
        h2t_done = sem("h2t_done")
        h2t_read = sem("h2t_read")
        rt_done = sem("rt_done")
        gl_ready = sem("gl_ready")
        mask_ready = sem("mask_ready")
        rank_done = sem("rank_done")
        gate_ready = sem("gate_ready")
        gt_done = sem("gt_done")
        gt_read = sem("gt_read")
        bd_done = sem("bd_done")
        acc_ready = sem("acc_ready")
        items_ready = sem("items_ready")
        sel_ready = sem("sel_ready")
        idx_done = sem("idx_done")
        idx_ready = sem("idx_ready")
        gathered = sem("gathered")
        xt_done = sem("xt_done")
        xt_ready = sem("xt_ready")
        gu_done = sem("gu_done")
        gu_used = sem("gu_used")
        g_ready = sem("g_ready")
        s_ready = sem("s_ready")
        act_ready = sem("act_ready")
        half_done = sem("half_done")
        down_done = sem("down_done")
        bias_ready = sem("bias_ready")
        rel_ready = sem("rel_ready")
        u_step = sem("u_step")
        now_ready = sem("now_ready")
        pad_step = sem("pad_step")
        paused = sem("paused")
        rt_read = sem("rt_read")
        msq_ready = sem("msq_ready")
        root_ready = sem("root_ready")
        y0_ready = sem("y0_ready")
        y1_ready = sem("y1_ready")
        scattered = sem("scattered")
        fin_in = sem("fin_in")
        ssf = sem("ssf")
        fin_ready = sem("fin_ready")
        stored = sem("stored")

        OFF_F = 3 * GW
        OFF_B = OFF_F + HEADS
        mix_cols = [OFF_B, OFF_B + GW, OFF_B + 2 * GW, 0, GW, 2 * GW]

        def mix_source(n):
            if n < 6:
                return w_in[:, mix_cols[n]:mix_cols[n] + GW].rearrange("(k p) c -> p k c", p=P)
            return w_out[:, (n - 6) * 512:(n - 5) * 512].rearrange("(k p) c -> p k c", p=P)

        def mix_tile(n):
            return part(ring[:, n % MIX_SLOTS, :], KD, 512)

        def gu_tile(q):
            return part(ring[:, q, :], KD, 512)

        def down_tile(h):
            return part(ring[:, 4 + h, :], 4, D)

        NU = 2 * HEADS * NT

        def tile_of(u):
            return u // 32, (u % 32) // NT, u % NT

        block = ctx.enter_context(nc.Block())

        @block.sync
        def _(sp):
            for n in range(MIX_PIECES):
                if n >= MIX_SLOTS:
                    sp.wait_ge(proj_done, 4 * (n - MIX_SLOTS + 1))
                sp.dma_start(mix_tile(n), mix_source(n)).then_inc(landed[n % MIX_SLOTS], 16)

            def load_item_piece(e, j):
                if j < 4:
                    src = w_gate_up[e, :, j * 512:(j + 1) * 512].rearrange("(k p) c -> p k c", p=P)
                    dst = gu_tile(j)
                else:
                    src = w_down[e, (j - 4) * 512:(j - 3) * 512, :].rearrange("(k p) c -> p k c", p=P)
                    dst = down_tile(j - 4)
                sp.dma_start(dst, src).then_inc(landed[j], 16)

            for j in (0, 1):
                sp.wait_ge(proj_done, 4 * (4 + j + 1))
                load_item_piece(0, j)
            sp.wait_ge(y_ready, 2 * HEADS)
            for j in (4, 5):
                load_item_piece(0, j)
            for j in (2, 3):
                sp.wait_ge(op_done, NT * (j - 1))
                load_item_piece(0, j)
            sp.wait_ge(items_ready, 1)
            n_items = sp.value_load(n_items_sb[0:1, 0:1], min_val=NE, max_val=NE + EXTRA_MAX)
            with sp.Fori(1, n_items) as i:
                e = sp.value_load(item_e[0:1, bass.ds(i, 1)], min_val=0, max_val=NE - 1)
                for j in range(6):
                    if j < 4:
                        sp.wait_ge(gu_done, i * 4 + (j - 3))
                    elif j == 4:
                        sp.wait_ge(half_done, i)
                    else:
                        sp.wait_ge(down_done, i)
                    if j < 4:
                        src = w_gate_up[bass.ds(e, 1), :, j * 512:(j + 1) * 512].rearrange(
                            "a (k p) c -> p (a k) c", p=P)
                        sp.dma_start(gu_tile(j), src).then_inc(landed[j], 16)
                    else:
                        src = w_down[bass.ds(e, 1), (j - 4) * 512:(j - 3) * 512, :].rearrange(
                            "a (k p) c -> p (a k) c", p=P)
                        sp.dma_start(down_tile(j - 4), src).then_inc(landed[j], 16)

        @block.gpsimd
        def _(pool):
            chain = [0]

            def link(ins):
                chain[0] += 1
                ins.then_inc(pstep, 1)
                pool.wait_ge(pstep, chain[0])

            def tri(dst, keep, fill, op, step, mult, width=P):
                link(nc.gpsimd.memset(dst, keep))
                return nc.gpsimd.affine_select(out=dst, in_=dst, compare_op=op, fill=fill, base=0,
                                               pattern=[[step, width]], channel_multiplier=mult)

            tri(ident[:], 0.0, 1.0, ALU.not_equal, -1, 1).then_inc(consts, 1)
            nc.gpsimd.memset(zrow, 0.0).then_inc(zero_ok, 1)
            tri(negtri, -1.0, 0.0, ALU.is_ge, 1, -1, SEQ).then_inc(consts, 1)
            tri(identb[:], 0.0, 1.0, ALU.not_equal, -1, 1).then_inc(consts, 1)
            tri(mask_strict[:], 0.0, NEG, ALU.is_gt, -1, 1).then_inc(consts, 1)
            tri(mask_causal[:], 0.0, NEG, ALU.is_ge, -1, 1).then_inc(consts, 1)
            tri(before[:], 1.0, 0.0, ALU.is_gt, 1, -1).then_inc(consts, 1)
            nc.gpsimd.memset(ones[:], 1.0).then_inc(consts, 1)
            nc.gpsimd.memset(onesrow[:], 1.0).then_inc(consts, 1)
            link(nc.gpsimd.memset(info[:], 1.0))
            nc.gpsimd.iota(iota[:], [[1, P]], base=0, channel_multiplier=0,
                           allow_small_or_imprecise_dtypes=True).then_inc(consts, 1)
            nc.gpsimd.iota(padrow[:], [[1, 1]], base=SEQ, channel_multiplier=1,
                           allow_small_or_imprecise_dtypes=True).then_inc(consts, 1)
            nc.gpsimd.iota(info[:, :, 0], [[P, NT]], base=0, channel_multiplier=1,
                           allow_small_or_imprecise_dtypes=True).then_inc(consts, 1)
            nc.gpsimd.iota(item_f[:], [[1, NI]], base=0, channel_multiplier=0,
                           allow_small_or_imprecise_dtypes=True).then_inc(consts, 1)
            nc.gpsimd.memset(item_b[:], -FAR).then_inc(consts, 1)
            nc.gpsimd.memset(pausing[:], 0.0).then_inc(paused, 1)
            pool.wait_ge(zero_ok, 1)
            pool.dma_start(acc_rows[SEQ:SEQ + P, :], zrow).then_inc(scattered, 16)

            def pause(c):
                nc.gpsimd.tensor_tensor(pausing[:, c:c + 1], onesrow[0:1, 0:1], onesrow[0:1, 0:1], ALU.add
                                        ).then_inc(paused, 1)

            def gather():
                pool.indirect_dma_start(out=xg, out_offset=None, in_=h2_rows,
                                        in_offset=bass.IndirectOffsetOnAxis(ap=idx_next[:, 0:1], axis=0)
                                        ).then_inc(gathered, 16)

            pool.wait_ge(items_ready, 1)
            n_items = pool.value_load(n_items_sb[0:1, 0:1], min_val=NE, max_val=NE + EXTRA_MAX)
            pool.wait_ge(h2_out, 16 * NT)
            pool.wait_ge(pads_out, 16)
            pool.wait_ge(idx_ready, 1)
            gather()
            pool.wait_ge(acc_out, 16 * NT)
            with pool.Fori(0, n_items) as i:
                pool.wait_ge(paused, i * 2 + 1)
                pool.wait_ge(idx_ready, i + 2)
                pool.wait_ge(xt_done, i + 1)
                pause(0)
                gather()
                pool.wait_ge(y0_ready, i + 2)
                pool.wait_ge(y1_ready, i + 2)
                pool.wait_ge(scattered, i * 16 + 16)
                pause(1)
                pool.indirect_dma_start(out=acc_rows, out_offset=bass.IndirectOffsetOnAxis(ap=idx_now[:, 0:1], axis=0),
                                        in_=ysb, in_offset=None, compute_op=ALU.add).then_inc(scattered, 16)
            pool.wait_ge(scattered, n_items * 16 + 16)

        @block.scalar
        def _(act):
            chain = [0]

            def link(ins):
                chain[0] += 1
                ins.then_inc(astep, 1)
                act.wait_ge(astep, chain[0])

            root_count = [0]

            def root(col, n):
                c = slice(col, col + n)
                root_count[0] += 1
                act.wait_ge(msq_ready, root_count[0])
                link(nc.scalar.activation(msq[:, c], msq[:, c], ACT.Ln))
                nc.scalar.activation(rstd[:, c], msq[:, c], ACT.Exp, scale=0.5).then_inc(root_ready, 1)

            nc.scalar.preload_act_table_set("natural_log_exp_and_others")
            xv = x[0].rearrange("(t p) d -> p t d", p=P)
            ov = out[0].rearrange("(t p) d -> p t d", p=P)
            for t in range(NT):
                act.dma_start(xres[:, t, :], xv[:, t, :]).then_inc(x_in[t], 16)
            with nc.allow_non_contiguous_dma(reason="gains, one per partition"):
                act.dma_start(g_attn[:], attn_norm_g.rearrange("(k p) -> p k", p=P)).then_inc(g_in, 16)
                act.dma_start(g_mix[:, 0:4], fox_out_g.rearrange("(k p) -> p k", p=P)).then_inc(g_in, 16)
                act.dma_start(g_mix[:, 4:8], sb_out_g.rearrange("(k p) -> p k", p=P)).then_inc(g_in, 16)
                act.dma_start(g_ffn[:], ffn_norm_g.rearrange("(k p) -> p k", p=P)).then_inc(g_in, 16)
                act.dma_start(w_f[:], w_in[:, OFF_F:OFF_F + HEADS].rearrange("(k p) c -> p k c", p=P)).then_inc(f_in, 16)
            act.dma_start(bf_b[:], b_forget.rearrange("(a h) -> a h", a=1).to_broadcast([P, HEADS])).then_inc(f_in, 16)
            act.dma_start(bgu_rows, b_gate_up).then_inc(bgu_in, 16)
            act.dma_start(w_r[:], w_router.rearrange("(k p) c -> p k c", p=P)).then_inc(r_in, 16)
            act.dma_start(br_b[:], b_router.rearrange("(a h) -> a h", a=1).to_broadcast([P, NE])).then_inc(r_in, 16)
            act.wait_ge(zero_ok, 1)
            act.dma_start(h2_rows[SEQ:SEQ + P, :], zrow).then_inc(pads_out, 16)

            for t in range(NT):
                act.wait_ge(x_in[t], 16)
                nc.scalar.activation(rows[:, t, :], xres[:, t, :], ACT.Square, accum_out=ssq[:, t:t + 1]).then_inc(ssx, 1)
                root(t, 1)

            act.wait_ge(g_in, 64)
            for k in range(0, KD, 2):
                act.wait_ge(tr_done, k + 1)
                nc.scalar.activation(colsT[:, k, :], pj_bank[0][:, :], ACT.Copy, scale=g_attn[:, k:k + 1]
                                     ).then_inc(tr_used_a, 1)

            act.wait_ge(zf_ready, 1)
            link(nc.scalar.activation(lf[:], zf[:], ACT.Abs))
            link(nc.scalar.activation(lf[:], lf[:], ACT.Exp, scale=-1.0))
            nc.scalar.activation(lf[:], lf[:], ACT.Ln, bias=1.0).then_inc(lf_abs, 1)

            def negc_copy():
                act.wait_ge(negc_ready, 1)
                act.dma_start(negc_rows, negc_sb[:]).then_inc(negc_out, 16)
                act.wait_ge(negc_out, 16)
                src = negc_rows.rearrange("(a h) s -> a (h s)", a=1).to_broadcast([P, HEADS * SEQ])
                act.dma_start(ring[:, 4, :], src).then_inc(negc_in, 16)

            def read_proj(n):
                act.wait_ge(proj_done, n + 1)
                ps = pj_bank[n % 2]
                g, c = n // 4, n % 4
                if g in (2, 5):
                    dst = v_sb[:, c, (GW if g == 2 else 0):(GW if g == 2 else 0) + GW]
                    ins = nc.scalar.copy(dst, ps[:, :])
                else:
                    slot = {0: 0, 1: 4, 3: 8, 4: 12}[g] + c
                    if g in (0, 3):
                        ins = nc.scalar.activation(qk[:, slot, :], ps[:, :], ACT.Copy, scale=SCALE)
                    else:
                        ins = nc.scalar.copy(qk[:, slot, :], ps[:, :])
                ins.then_inc(proj_read, 1)

            def soft(u):
                g, h, t = tile_of(u)
                w = (t + 1) * P
                act.wait_ge(score_done, u + 1)
                if u == 0:
                    act.wait_ge(pads_out, 16)
                    act.wait_ge(scattered, 16)
                    act.wait_ge(cum_done, 1)
                if u >= 2:
                    act.wait_ge(arg_ready, u - 1)
                link(nc.scalar.activation(wk[:, u % 2, 0:w], sc_bank[u % 2][:, 0:w], ACT.Abs))
                link(nc.scalar.activation(wk[:, u % 2, 0:w], wk[:, u % 2, 0:w], ACT.Exp, scale=-1.0))
                nc.scalar.activation(wk[:, u % 2, 0:w], wk[:, u % 2, 0:w], ACT.Ln, bias=1.0).then_inc(softln, 1)

            def prob(u):
                g, h, t = tile_of(u)
                w = (t + 1) * P
                act.wait_ge(arg_ready, u + 1)
                if g == 0:
                    nc.scalar.activation(wk[:, 4 + u % 2, 0:w], wk[:, 4 + u % 2, 0:w], ACT.Exp).then_inc(prob_ready, 1)
                else:
                    c = u - 32
                    nc.scalar.activation(wk[:, 4 + u % 2, 0:w], wk[:, 4 + u % 2, 0:w], ACT.Exp, scale=-1.0,
                                         bias=nmax[:, c:c + 1], accum_out=rsum[:, c:c + 1]).then_inc(prob_ready, 1)

            def copy_probT(u):
                g, h, t = tile_of(u)
                w = (t + 1) * P
                act.wait_ge(probT_done, u + 1)
                act.wait_ge(pv_done, u - 1)
                nc.scalar.copy(wk[:, 6 + u % 2, 0:w], pt_bank[u % 2][:, 0:w]).then_inc(probT_a, 1)

            for n in range(8):
                read_proj(n)
                if n == 3:
                    negc_copy()
            for n in range(NU // 2 + 3):
                if n < 16:
                    read_proj(8 + n)
                if 2 * n < 32:
                    soft(2 * n)
                if 1 <= n and 2 * n - 1 < NU:
                    prob(2 * n - 1)
                if 2 * n < 32:
                    soft(2 * n + 1)
                if 2 * n < NU:
                    prob(2 * n)
                for u in (2 * n - 2, 2 * n - 1):
                    if 32 <= u < NU:
                        copy_probT(u)

            for g in range(2):
                act.wait_ge(y_ready, HEADS * (g + 1))
                for t in range(NT):
                    c = (4 if g == 0 else 8) + t
                    o = GW if g == 0 else 0
                    act.wait_ge(proj_done, 24)
                    nc.scalar.activation(colsT[:, t, :], rows[:, t, o:o + GW], ACT.Square,
                                         accum_out=ssq[:, c:c + 1]).then_inc(ssy, 1)
                root(4 if g == 0 else 8, 4)
            act.dma_start(bdown_sb, b_down).then_inc(bdown_in, 16)

            for t in range(NT):
                act.wait_ge(x1_ready, NT + t + 1)
                act.wait_ge(yn_ready, 2 * NT)
                act.wait_ge(yt_done, KD)
                nc.scalar.activation(rows[:, t, :], xres[:, t, :], ACT.Square,
                                     accum_out=ssq[:, 12 + t:13 + t]).then_inc(ss1, 1)
                root(12 + t, 1)
                act.wait_ge(h2_ready, t + 1)
                act.dma_start(h2_rows[t * P:(t + 1) * P, :], rows[:, t, :]).then_inc(h2_out, 16)

            act.wait_ge(gl_ready, 1)
            nc.scalar.activation(gexp[:], gexp[:], ACT.Exp).then_inc(y0_ready, 1)
            for t in range(NT):
                act.wait_ge(acc_ready, 2 * (t + 1))
                act.dma_start(acc_rows[t * P:(t + 1) * P, :], xres[:, t, :]).then_inc(acc_out, 16)

            act.wait_ge(items_ready, 1)
            n_items = act.value_load(n_items_sb[0:1, 0:1], min_val=NE, max_val=NE + EXTRA_MAX)
            with act.Fori(0, n_items) as i:
                for q in range(4):
                    act.wait_ge(g_ready, i * 4 + (q + 1))
                    nc.scalar.activation(stile[q % 2], gtile[q % 2], ACT.Sigmoid, scale=ALPHA).then_inc(s_ready, 1)
                act.wait_ge(down_done, i + 1)
                act.wait_ge(idx_ready, i + 2)
                act.wait_ge(scattered, i * 16 + 16)
                nc.scalar.activation(ysb[:, 0:512], pv_bank[0][0:BLK, :], ACT.Copy, scale=gate_now[:, 0:1]
                                     ).then_inc(y0_ready, 1)

            nc.scalar.preload_act_table_set("natural_log_exp_and_others")
            act.dma_start(fing, final_norm_g.rearrange("(a d) -> a d", a=1).to_broadcast([P, D])).then_inc(fing_in, 16)
            act.wait_ge(scattered, n_items * 16 + 16)
            for t in range(NT):
                act.dma_start(xres[:, t, :], acc_rows[t * P:(t + 1) * P, :]).then_inc(x_in[t], 16)
            for t in range(NT):
                act.wait_ge(x_in[t], 32)
                nc.scalar.activation(rows[:, t, :], xres[:, t, :], ACT.Square, accum_out=ssq[:, t:t + 1]).then_inc(ssf, 1)
                root(t, 1)
            for t in range(NT):
                act.wait_ge(fin_ready, t + 1)
                act.dma_start(ov[:, t, :], rows[:, t, :]).then_inc(stored, 16)
            act.wait_ge(stored, 16 * NT)

        @block.vector
        def _(dve):
            chain = [0]

            def link(ins):
                chain[0] += 1
                ins.then_inc(dstep, 1)
                dve.wait_ge(dstep, chain[0])

            rms_count = [0]

            def rms(col, n, width):
                c = slice(col, col + n)
                nc.vector.tensor_scalar(msq[:, c], ssq[:, c], 1.0 / width, EPS, ALU.mult, ALU.add).then_inc(msq_ready, 1)
                rms_count[0] += 1
                dve.wait_ge(root_ready, rms_count[0])
                link(nc.vector.reciprocal(rstd[:, c], rstd[:, c]))

            for t in range(NT):
                dve.wait_ge(ssx, t + 1)
                rms(t, 1, D)
                nc.vector.tensor_scalar(rows[:, t, :], xres[:, t, :], rstd[:, t:t + 1], None, ALU.mult
                                        ).then_inc(xn_ready, 1)
            dve.wait_ge(bgu_done, 1)
            nc.vector.tensor_copy(bgu[:].rearrange("p e c -> p c e"), pt_bank[0][:, :].rearrange("p (c e) -> p c e", e=NE)
                                  ).then_inc(bgu_read, 1)
            dve.wait_ge(g_in, 64)
            for k in range(1, KD, 2):
                dve.wait_ge(tr_done, k + 1)
                nc.vector.tensor_scalar(colsT[:, k, :], pj_bank[1][:, :], g_attn[:, k:k + 1], None, ALU.mult
                                        ).then_inc(tr_used_v, 1)
            dve.wait_ge(f_in, 32)
            dve.wait_ge(f_done, 1)
            nc.vector.tensor_tensor(zf[:], pt_bank[1][:, 0:NT * HEADS].rearrange("p (t h) -> p t h", h=HEADS),
                                    bf_b[:].rearrange("p (a h) -> p a h", a=1).to_broadcast([P, NT, HEADS]), ALU.add
                                    ).then_inc(zf_ready, 1)
            dve.wait_ge(lf_abs, 1)
            nc.vector.scalar_tensor_tensor(out=lf[:], in0=zf[:], scalar=0.0, in1=lf[:], op0=ALU.min, op1=ALU.subtract
                                           ).then_inc(lf_ready, 1)
            dve.wait_ge(cum_done, 1)
            nc.vector.tensor_copy(negc_sb[:], pt_bank[1][0:HEADS, :]).then_inc(negc_ready, 1)

            def arg(u):
                g, h, t = tile_of(u)
                w = (t + 1) * P
                if g == 0:
                    dve.wait_ge(softln, u + 1)
                    z = sc_bank[u % 2][:, 0:w]
                    link(nc.vector.scalar_tensor_tensor(out=wk[:, 2, 0:w], in0=z, scalar=0.0, in1=wk[:, u % 2, 0:w],
                                                        op0=ALU.max, op1=ALU.add))
                    link(nc.vector.tensor_tensor_scan(out=wk[:, 3, w - 1::-1], data0=onesrow[:, 0:1].to_broadcast([P, w]),
                                                      data1=wk[:, 2, w - 1::-1], initial=0.0,
                                                      op0=ALU.mult, op1=ALU.add))
                    if u >= 2:
                        dve.wait_ge(probT_done, u - 1)
                    nc.vector.tensor_tensor(wk[:, 4 + u % 2, 0:w], z, wk[:, 3, 0:w], ALU.subtract).then_inc(arg_ready, 1)
                else:
                    c = u - 32
                    dve.wait_ge(score_done, u + 1)
                    if c == 0:
                        dve.wait_ge(negc_in, 16)
                    dve.wait_ge(probT_done, u - 1)
                    nc.vector.tensor_tensor_reduce(out=wk[:, 4 + u % 2, 0:w], in0=sc_bank[u % 2][:, 0:w],
                                                   in1=negc[:, h, 0:w], scale=-1.0, scalar=3e38, op0=ALU.add,
                                                   op1=ALU.min, accum_out=nmax[:, c:c + 1]).then_inc(arg_ready, 1)

            def copy_probT(u):
                g, h, t = tile_of(u)
                w = (t + 1) * P
                dve.wait_ge(probT_done, u + 1)
                if u >= 2:
                    dve.wait_ge(pv_done, u - 1)
                nc.vector.tensor_copy(wk[:, 6 + u % 2, 0:w], pt_bank[u % 2][:, 0:w]).then_inc(probT_v, 1)

            def read_y(hh):
                g, h = hh // HEADS, hh % HEADS
                dve.wait_ge(pv_done, 4 * (hh + 1))
                ps = pv_bank[hh % 2][:, 0:NT * DH].rearrange("p (t d) -> p t d", d=DH)
                o = (GW if g == 0 else 0) + h * DH
                if g == 0:
                    nc.vector.tensor_copy(rows[:, :, o:o + DH], ps).then_inc(y_ready, 1)
                else:
                    link(nc.vector.reciprocal(rinv[:, 4 * h:4 * h + 4], rsum[:, 4 * h:4 * h + 4]))
                    nc.vector.tensor_tensor(rows[:, :, o:o + DH], ps,
                                            rinv[:, 4 * h:4 * h + 4].rearrange("p (t a) -> p t a", a=1)
                                            .to_broadcast([P, NT, DH]), ALU.mult).then_inc(y_ready, 1)

            def norm_y(g):
                dve.wait_ge(ssy, 4 * (g + 1))
                c0, o = (4, GW) if g == 0 else (8, 0)
                rms(c0, 4, GW)
                for t in range(NT):
                    nc.vector.tensor_scalar(rows[:, t, o:o + GW], rows[:, t, o:o + GW], rstd[:, c0 + t:c0 + t + 1],
                                            None, ALU.mult).then_inc(yn_ready, 1)

            dve.wait_ge(tr_done, KD)
            for n in range(NU // 2 + 3):
                for u in (2 * n, 2 * n + 1):
                    if u < NU:
                        arg(u)
                for u in (2 * n - 2, 2 * n - 1):
                    if 0 <= u < 32:
                        copy_probT(u)
                if n >= 4 and (n - 4) % 2 == 0 and (n - 4) // 2 < 2 * HEADS:
                    read_y((n - 4) // 2)
            norm_y(0)
            norm_y(1)
            for k in range(KD):
                dve.wait_ge(yt_done, k + 1)
                nc.vector.tensor_scalar(colsT[:, k, :], pt_bank[k % 2][:, :], g_mix[:, k:k + 1], None, ALU.mult
                                        ).then_inc(yt_read, 1)

            def read_op(m):
                half, t = m // NT, m % NT
                dve.wait_ge(op_done, m + 1)
                nc.vector.tensor_tensor(xres[:, t, half * 512:half * 512 + 512], pj_bank[m % 2][:, :],
                                        xres[:, t, half * 512:half * 512 + 512], ALU.add).then_inc(x1_ready, 1)

            def norm_1(t):
                dve.wait_ge(ss1, t + 1)
                rms(12 + t, 1, D)
                nc.vector.tensor_scalar(rows[:, t, :], xres[:, t, :], rstd[:, 12 + t:13 + t], None, ALU.mult
                                        ).then_inc(h2_ready, 1)

            def read_h2t(t):
                for hf in range(2):
                    dve.wait_ge(h2t_done, 2 * t + hf + 1)
                    nc.vector.tensor_tensor(h2T[:, 4 * hf:4 * hf + 4, t * P:(t + 1) * P],
                                            pt_bank[hf][:, :].rearrange("p (k c) -> p k c", c=P),
                                            g_ffn[:, 4 * hf:4 * hf + 4].rearrange("p (k a) -> p k a", a=1)
                                            .to_broadcast([P, 4, P]), ALU.mult).then_inc(h2t_read, 1)

            def route(t):
                dve.wait_ge(r_in, 32)
                dve.wait_ge(rt_done, t + 1)
                nc.vector.tensor_tensor(logits[:, t, :], sc_bank[t % 2][:, 0:NE], br_b[:], ALU.add).then_inc(rt_read, 1)
                dve.wait_ge(rt_read, t + 1)
                link(nc.vector.max(top8[:, t, :], logits[:, t, :]))
                link(nc.vector.max_index(topi[:, t, :], top8[:, t, :], logits[:, t, :]))

            for m in range(2 * NT):
                read_op(m)
                if m > NT:
                    norm_1(m - NT - 1)
                if m > NT + 1:
                    read_h2t(m - NT - 2)
            norm_1(NT - 1)
            read_h2t(NT - 2)
            route(0)
            read_h2t(NT - 1)
            for t in range(1, NT):
                route(t)

            nc.vector.tensor_tensor(gexp[:], top8[:, :, 0:TOPK], top8[:, :, 0:1].to_broadcast([P, NT, TOPK]),
                                    ALU.subtract).then_inc(gl_ready, 1)
            link(nc.vector.tensor_copy(topf[:], topi[:]))
            dve.wait_ge(consts, 13)
            link(nc.vector.tensor_tensor(
                onehot, iota[:, 0:NE].rearrange("p (a b e) -> p a b e", a=1, b=1).to_broadcast([P, NT, TOPK, NE]),
                topf[:, :, 0:TOPK].rearrange("p t (k a) -> p t k a", a=1).to_broadcast([P, NT, TOPK, NE]), ALU.is_equal))
            link(nc.vector.tensor_reduce(maskf[:], onehot.rearrange("p t k e -> p t e k"), AX.X, ALU.add))
            nc.vector.tensor_copy(maskb[:], maskf[:]).then_inc(mask_ready, 1)
            dve.wait_ge(y0_ready, 1)
            link(nc.vector.tensor_reduce(gsum[:], gexp[:], AX.X, ALU.add))
            link(nc.vector.reciprocal(ginv[:], gsum[:]))
            link(nc.vector.tensor_tensor(gexp[:], gexp[:], ginv[:].rearrange("p (t a) -> p t a", a=1)
                                         .to_broadcast([P, NT, TOPK]), ALU.mult))
            link(nc.vector.tensor_tensor(onehot_g, onehot, gexp[:].rearrange("p t (k a) -> p t k a", a=1)
                                         .to_broadcast([P, NT, TOPK, NE]), ALU.mult))
            nc.vector.tensor_reduce(gate_et[:].rearrange("p (e t) -> p t e", t=NT),
                                    onehot_g.rearrange("p t k e -> p t e k"), AX.X, ALU.add).then_inc(gate_ready, 1)
            dve.wait_ge(rank_done, 1)
            link(nc.vector.scalar_tensor_tensor(
                out=rank_et[:].rearrange("p (e t) -> p t e", t=NT), in0=maskf[:], scalar=-FAR,
                in1=pj_bank[0][:, 0:NT * NE].rearrange("p (t e) -> p t e", e=NE), op0=ALU.mult, op1=ALU.add))
            link(nc.vector.tensor_copy(counts[:], pj_bank[0][:, NT * NE:(NT + 1) * NE]))
            link(nc.vector.tensor_scalar(extra[:], counts[:], float(BLK), None, ALU.is_gt))
            for b in range(2, MAXBLK):
                link(nc.vector.scalar_tensor_tensor(out=extra[:], in0=counts[:], scalar=float(b * BLK), in1=extra[:],
                                                    op0=ALU.is_gt, op1=ALU.add))
            link(nc.vector.tensor_tensor_scan(out=cumx[:], data0=onesrow[:], data1=extra[:], initial=0.0,
                                              op0=ALU.mult, op1=ALU.add))
            link(nc.vector.tensor_scalar(n_items_sb[:], cumx[0:1, NE - 1:NE], float(NE), None, ALU.add))
            cum_b = cumx[:].rearrange("p (a e) -> p a e", a=1).to_broadcast([P, NX, NE])
            ext_b = extra[:].rearrange("p (a e) -> p a e", a=1).to_broadcast([P, NX, NE])
            j_b = iota[:, 0:NX].rearrange("p (j a) -> p j a", a=1).to_broadcast([P, NX, NE])
            link(nc.vector.tensor_tensor(itemcmp, cum_b, j_b, ALU.is_le))
            link(nc.vector.tensor_tensor(itemcmp2, itemcmp, ext_b, ALU.mult))
            link(nc.vector.tensor_reduce(item_f[:, NE:NI], itemcmp, AX.X, ALU.add))
            link(nc.vector.tensor_scalar(item_f[:, NE:NI], item_f[:, NE:NI], float(NE - 1), None, ALU.min))
            link(nc.vector.tensor_reduce(cxj[:], itemcmp2, AX.X, ALU.add))
            link(nc.vector.tensor_tensor(cxj[:], iota[:, 0:NX], cxj[:], ALU.subtract))
            link(nc.vector.tensor_scalar(item_b[:, NE:NI], cxj[:], float(BLK), float(BLK) - FAR, ALU.mult, ALU.add))
            nc.vector.tensor_copy(item_e[:], item_f[0:1, :]).then_inc(items_ready, 1)
            dve.wait_ge(items_ready, 1)

            def build_sel():
                link(nc.vector.tensor_scalar(rel[:], rank_et[:, 0:NT], item_b[:, 0:1], None, ALU.subtract))
                nc.vector.tensor_copy(info[:, :, 2], gate_et[:, 0:NT]).then_inc(gu_used, 2)
                for t in range(NT):
                    ins = nc.vector.tensor_scalar(sel[:, t, :], iota[:, 0:BLK], rel[:, t:t + 1], None, ALU.is_equal)
                ins.then_inc(sel_ready, 1)

            def read_idx():
                ps = pj_bank[0]
                nc.vector.tensor_copy(gate_next[:], ps[0:BLK, 2:3])
                link(nc.vector.tensor_scalar(padsel[:], ps[0:BLK, 1:2], 0.0, padrow[0:BLK, 0:1], ALU.is_equal, ALU.mult))
                nc.vector.tensor_tensor(idx_next[:], padsel[:], ps[0:BLK, 0:1], ALU.add).then_inc(idx_ready, 1)

            def read_xt():
                for hf in range(2):
                    ins = nc.vector.tensor_tensor(
                        xgT[:, 4 * hf:4 * hf + 4, :], pt_bank[hf][:, 0:4 * BLK].rearrange("p (k c) -> p k c", c=BLK),
                        g_ffn[:, 4 * hf:4 * hf + 4].rearrange("p (k a) -> p k a", a=1).to_broadcast([P, 4, BLK]),
                        ALU.mult)
                ins.then_inc(xt_ready, 1)

            build_sel()
            dve.wait_ge(gt_done, 1)
            nc.vector.tensor_copy(gT, pt_bank[0][0:NE, :]).then_inc(gt_read, 1)
            dve.wait_ge(idx_done, 1)
            read_idx()
            for m in range(2 * NT):
                t, half = m // 2, m % 2
                dve.wait_ge(bd_done, m + 1)
                nc.vector.tensor_tensor(xres[:, t, half * 512:half * 512 + 512], sc_bank[m % 2][:, :],
                                        xres[:, t, half * 512:half * 512 + 512], ALU.add).then_inc(acc_ready, 1)
            dve.wait_ge(xt_done, 1)
            read_xt()
            nc.vector.memset(biasc[:], 0.0).then_inc(y1_ready, 1)
            dve.wait_ge(y1_ready, 1)
            dve.wait_ge(acc_ready, 2 * NT)

            n_items = dve.value_load(n_items_sb[0:1, 0:1], min_val=NE, max_val=NE + EXTRA_MAX)
            with dve.Fori(0, n_items) as i:
                e_now = dve.value_load(item_e[0:1, bass.ds(i, 1)], min_val=0, max_val=NE - 1)
                e_next = dve.value_load(item_e[0:1, bass.ds(i + 1, 1)], min_val=0, max_val=NE - 1)
                nc.vector.tensor_copy(biasc[:], bgu[:].rearrange("p e c -> p (e c)")[:, bass.ds(e_now * 16, 16)]
                                      ).then_inc(bias_ready, 1)
                dve.wait_ge(idx_done, i + 1)
                nc.vector.tensor_scalar(rel[:], rank_et[:, bass.ds(e_next * NT, NT)], item_b[:, bass.ds(i + 1, 1)],
                                        None, ALU.subtract).then_inc(rel_ready, 1)
                nc.vector.tensor_copy(info[:, :, 2], gate_et[:, bass.ds(e_next * NT, NT)])
                dve.wait_ge(rel_ready, i + 1)
                for t in range(NT):
                    ins = nc.vector.tensor_scalar(sel[:, t, :], iota[:, 0:BLK], rel[:, t:t + 1], None, ALU.is_equal)
                ins.then_inc(sel_ready, 1)
                dve.wait_ge(bias_ready, i + 1)
                for q in range(4):
                    gt, ut, st, ps = gtile[q % 2], utile[q % 2], stile[q % 2], sc_bank[q % 2]
                    dve.wait_ge(gu_done, i * 4 + (q + 1))
                    for jj in range(2):
                        c = 4 * q + 2 * jj
                        gi = nc.vector.tensor_scalar(gt[:, jj, :], ps[:, (2 * jj) * BLK:(2 * jj + 1) * BLK],
                                                     biasc[:, c:c + 1], LIMIT, ALU.add, ALU.min)
                    gi.then_inc(g_ready, 1)
                    for jj in range(2):
                        c = 4 * q + 2 * jj + 1
                        ui = nc.vector.tensor_scalar(ut[:, jj, :], ps[:, (2 * jj + 1) * BLK:(2 * jj + 2) * BLK],
                                                     biasc[:, c:c + 1], LIMIT, ALU.add, ALU.min)
                    ui.then_inc(gu_used, 1)
                    dve.wait_ge(gu_used, i * 4 + (q + 3))
                    nc.vector.tensor_scalar(ut, ut, -LIMIT, 1.0, ALU.max, ALU.add).then_inc(u_step, 1)
                    dve.wait_ge(u_step, i * 8 + (2 * q + 1))
                    dve.wait_ge(g_ready, i * 4 + (q + 1))
                    nc.vector.tensor_tensor(ut, gt, ut, ALU.mult).then_inc(u_step, 1)
                    dve.wait_ge(u_step, i * 8 + (2 * q + 2))
                    dve.wait_ge(s_ready, i * 4 + (q + 1))
                    nc.vector.tensor_tensor(actT[:, 2 * q:2 * q + 2, :], ut, st, ALU.mult).then_inc(act_ready, 1)
                    if q == 0:
                        dve.wait_ge(scattered, i * 16 + 16)
                        nc.vector.tensor_copy(gate_now[:], gate_next[:])
                        nc.vector.tensor_copy(idx_now[:], idx_next[:]).then_inc(now_ready, 1)
                        dve.wait_ge(now_ready, i + 1)
                        dve.wait_ge(idx_done, i + 2)
                        ps0 = pj_bank[0]
                        nc.vector.tensor_copy(gate_next[:], ps0[0:BLK, 2:3])
                        nc.vector.tensor_scalar(padsel[:], ps0[0:BLK, 1:2], 0.0, padrow[0:BLK, 0:1], ALU.is_equal,
                                                ALU.mult).then_inc(pad_step, 1)
                        dve.wait_ge(pad_step, i + 1)
                        nc.vector.tensor_tensor(idx_next[:], padsel[:], ps0[0:BLK, 0:1], ALU.add).then_inc(idx_ready, 1)
                dve.wait_ge(xt_done, i + 2)
                read_xt()
                dve.wait_ge(down_done, i + 1)
                nc.vector.tensor_scalar(ysb[:, 512:D], pv_bank[1][0:BLK, :], gate_now[:, 0:1], None, ALU.mult
                                        ).then_inc(y1_ready, 1)

            for t in range(NT):
                dve.wait_ge(ssf, t + 1)
                rms(t, 1, D)
                dve.wait_ge(fing_in, 16)
                nc.vector.scalar_tensor_tensor(out=rows[:, t, :], in0=xres[:, t, :], scalar=rstd[:, t:t + 1], in1=fing,
                                               op0=ALU.mult, op1=ALU.mult).then_inc(fin_ready, 1)

        @block.tensor
        def _(pe):
            pe.wait_ge(consts, 1)
            pe.wait_ge(bgu_in, 16)
            for c in range(16):
                q, r = c // 2, c % 2
                last = nc.tensor.transpose(pt_bank[0][:, c * NE:(c + 1) * NE],
                                           bgu_rows[:, q * 256 + r:q * 256 + r + 255:2], ident[0:NE, 0:NE])
            last.then_inc(bgu_done, 1)
            pe.wait_ge(xn_ready, NT)
            for k in range(KD):
                if k >= 2:
                    pe.wait_ge(tr_used_a if k % 2 == 0 else tr_used_v, k // 2)
                for t in range(NT):
                    last = nc.tensor.transpose(pj_bank[k % 2][:, t * P:(t + 1) * P], rows[:, t, k * P:(k + 1) * P],
                                               ident[:])
                last.then_inc(tr_done, 1)
            pe.wait_ge(tr_used_a, KD // 2)
            pe.wait_ge(tr_used_v, KD // 2)
            pe.wait_ge(f_in, 32)
            for t in range(NT):
                for k in range(KD):
                    last = nc.tensor.matmul(pt_bank[1][:, t * HEADS:(t + 1) * HEADS], colsT[:, k, t * P:(t + 1) * P],
                                            w_f[:, k, :], start=(k == 0), stop=(k == KD - 1))
            last.then_inc(f_done, 1)

            def project(n):
                g, c = n // 4, n % 4
                w = mix_tile(g)
                if c == 0:
                    pe.wait_ge(landed[g % MIX_SLOTS], 16 * (g // MIX_SLOTS + 1))
                if n >= 2:
                    pe.wait_ge(proj_read, n - 1)
                ps = pj_bank[n % 2]
                for k in range(KD):
                    if g in (2, 5):
                        last = nc.tensor.matmul(ps[:, :], colsT[:, k, c * P:(c + 1) * P], w[:, k, :],
                                                start=(k == 0), stop=(k == KD - 1))
                    else:
                        last = nc.tensor.matmul(ps[:, :], w[:, k, c * P:(c + 1) * P], colsT[:, k, :],
                                                start=(k == 0), stop=(k == KD - 1))
                last.then_inc(proj_done, 1)

            def score(u):
                g, h, t = tile_of(u)
                w = (t + 1) * P
                base = 0 if g == 0 else 8
                lo = (h % 2) * DH
                if u == 0:
                    pe.wait_ge(proj_read, 8)
                    pe.wait_ge(consts, 13)
                if u == 32:
                    pe.wait_ge(proj_read, 20)
                if u >= 2:
                    pe.wait_ge(arg_ready, u - 1)
                ps = sc_bank[u % 2]
                q = qk[lo:lo + DH, base + h // 2, t * P:(t + 1) * P]
                if t > 0:
                    nc.tensor.matmul(ps[:, 0:t * P], q, qk[lo:lo + DH, base + 4 + h // 2, 0:t * P], start=True, stop=True)
                nc.tensor.matmul(ps[:, t * P:w], q, qk[lo:lo + DH, base + 4 + h // 2, t * P:w], start=True, stop=False)
                nc.tensor.matmul(ps[:, t * P:w], identb[:], (mask_strict if g == 0 else mask_causal)[:],
                                 start=False, stop=True).then_inc(score_done, 1)

            def transpose_prob(u):
                g, h, t = tile_of(u)
                pe.wait_ge(prob_ready, u + 1)
                if u >= 2:
                    if u - 2 < 32:
                        pe.wait_ge(probT_v, u - 1)
                    else:
                        pe.wait_ge(probT_a, u - 33)
                for s in range(t + 1):
                    last = nc.tensor.transpose(pt_bank[u % 2][:, s * P:(s + 1) * P],
                                               wk[:, 4 + u % 2, s * P:(s + 1) * P], ident[:])
                last.then_inc(probT_done, 1)

            def attend(u):
                g, h, t = tile_of(u)
                hh = u // NT
                if u < 32:
                    pe.wait_ge(probT_v, u + 1)
                else:
                    pe.wait_ge(probT_a, u - 31)
                if t == 0 and hh >= 2:
                    pe.wait_ge(y_ready, hh - 1)
                pe.wait_ge(proj_read, 8 + t + 1 if g == 0 else 20 + t + 1)
                o = (GW if g == 0 else 0) + h * DH
                for s in range(t + 1):
                    last = nc.tensor.matmul(pv_bank[hh % 2][:, t * DH:(t + 1) * DH], wk[:, 6 + u % 2, s * P:(s + 1) * P],
                                            v_sb[:, s, o:o + DH], start=(s == 0), stop=(s == t))
                last.then_inc(pv_done, 1)

            for n in range(8):
                project(n)
                if n == 0:
                    pe.wait_ge(lf_ready, 1)
                    pe.wait_ge(consts, 2)
                    for t in range(NT):
                        last = nc.tensor.matmul(pt_bank[1][0:HEADS, t * P:SEQ], lf[:, t, :], negtri[:, 0:SEQ - t * P],
                                                start=(t == 0), stop=(t == NT - 1))
                    last.then_inc(cum_done, 1)
            for n in range(NU // 2 + 3):
                if n < 16:
                    project(8 + n)
                for u in (2 * n, 2 * n + 1):
                    if u < NU:
                        score(u)
                for u in (2 * n - 2, 2 * n - 1):
                    if 0 <= u < NU:
                        if u == 0:
                            pe.wait_ge(bgu_read, 1)
                            pe.wait_ge(negc_ready, 1)
                        transpose_prob(u)
                for u in (2 * n - 4, 2 * n - 3):
                    if 0 <= u < NU:
                        attend(u)

            pe.wait_ge(yn_ready, 2 * NT)
            for k in range(KD):
                if k >= 2:
                    pe.wait_ge(yt_read, k - 1)
                for t in range(NT):
                    last = nc.tensor.transpose(pt_bank[k % 2][:, t * P:(t + 1) * P], rows[:, t, k * P:(k + 1) * P],
                                               ident[:])
                last.then_inc(yt_done, 1)

            def project_out(m):
                half, t = m // NT, m % NT
                if t == 0:
                    n = 6 + half
                    pe.wait_ge(landed[n % MIX_SLOTS], 16 * (n // MIX_SLOTS + 1))
                if m == 0:
                    pe.wait_ge(yt_read, KD)
                if m >= 2:
                    pe.wait_ge(x1_ready, m - 1)
                w = mix_tile(6 + half)
                for k in range(KD):
                    last = nc.tensor.matmul(pj_bank[m % 2][:, :], colsT[:, k, t * P:(t + 1) * P], w[:, k, :],
                                            start=(k == 0), stop=(k == KD - 1))
                last.then_inc(op_done, 1)

            def transpose_h2(t):
                pe.wait_ge(h2_ready, t + 1)
                for hf in range(2):
                    if t >= 1:
                        pe.wait_ge(h2t_read, 2 * t - 1 + hf)
                    for k in range(4):
                        kk = 4 * hf + k
                        last = nc.tensor.transpose(pt_bank[hf][:, k * P:(k + 1) * P], rows[:, t, kk * P:(kk + 1) * P],
                                                   ident[:])
                    last.then_inc(h2t_done, 1)

            def router(t):
                pe.wait_ge(h2t_read, 2 * t + 2)
                pe.wait_ge(r_in, 32)
                if t >= 2:
                    pe.wait_ge(rt_read, t - 1)
                for k in range(KD):
                    last = nc.tensor.matmul(sc_bank[t % 2][:, 0:NE], h2T[:, k, t * P:(t + 1) * P], w_r[:, k, :],
                                            start=(k == 0), stop=(k == KD - 1))
                last.then_inc(rt_done, 1)

            for m in range(2 * NT):
                project_out(m)
                if m > NT:
                    transpose_h2(m - NT - 1)
            transpose_h2(NT - 1)
            for t in range(NT):
                router(t)

            pe.wait_ge(mask_ready, 1)
            pe.wait_ge(x1_ready, 2 * NT)
            for t in range(NT + 1):
                top = min(t, NT - 1)
                for s in range(top + 1):
                    last = nc.tensor.matmul(pj_bank[0][:, t * NE:(t + 1) * NE], (before if s == t else ones)[:],
                                            maskb[:, s, :], start=(s == 0), stop=(s == top))
            last.then_inc(rank_done, 1)
            pe.wait_ge(gate_ready, 1)
            pe.wait_ge(h2t_read, 2 * NT)
            gv = gate_et[:].rearrange("p (e t) -> p t e", t=NT)
            for t in range(NT):
                last = nc.tensor.transpose(pt_bank[0][0:NE, t * P:(t + 1) * P], gv[:, t, :], ident[:])
            last.then_inc(gt_done, 1)

            def slot_rows():
                for t in range(NT):
                    last = nc.tensor.matmul(pj_bank[0][0:BLK, 0:4], sel[:, t, :], info[:, t, :],
                                            start=(t == 0), stop=(t == NT - 1))
                last.then_inc(idx_done, 1)

            def transpose_x():
                for k in range(KD):
                    hf, kk = k // 4, k % 4
                    last = nc.tensor.transpose(pt_bank[hf][:, kk * BLK:(kk + 1) * BLK], xg[:, k * P:(k + 1) * P],
                                               ident[0:BLK, 0:BLK])
                last.then_inc(xt_done, 1)

            pe.wait_ge(sel_ready, 1)
            slot_rows()
            pe.wait_ge(gt_read, 1)
            pe.wait_ge(bdown_in, 16)
            for m in range(2 * NT):
                t, half = m // 2, m % 2
                if m >= 2:
                    pe.wait_ge(acc_ready, m - 1)
                nc.tensor.matmul(sc_bank[m % 2][:, :], gT[:, t * P:(t + 1) * P], bdown_sb[:, half * 512:half * 512 + 512],
                                 start=True, stop=True).then_inc(bd_done, 1)
            pe.wait_ge(gathered, 16)
            transpose_x()
            pe.wait_ge(acc_ready, 2 * NT)

            n_items = pe.value_load(n_items_sb[0:1, 0:1], min_val=NE, max_val=NE + EXTRA_MAX)
            with pe.Fori(0, n_items) as i:
                pe.wait_ge(xt_ready, i + 1)
                for q in range(4):
                    pe.wait_ge(landed[q], i * 16 + 48)
                    pe.wait_ge(gu_used, i * 4 + (q + 1))
                    w = gu_tile(q)
                    for jj in range(2):
                        for r in range(2):
                            o = (2 * jj + r) * BLK
                            for k in range(KD):
                                last = nc.tensor.matmul(sc_bank[q % 2][:, o:o + BLK],
                                                        w[:, k, jj * 256 + r:jj * 256 + r + 255:2], xgT[:, k, :],
                                                        start=(k == 0), stop=(k == KD - 1))
                    last.then_inc(gu_done, 1)
                    if q == 0:
                        pe.wait_ge(sel_ready, i + 2)
                        slot_rows()
                for k in range(KD):
                    if k % 4 == 0:
                        pe.wait_ge(landed[4 + k // 4], i * 16 + 16)
                    if k % 2 == 0:
                        pe.wait_ge(act_ready, i * 4 + (k // 2 + 1))
                    if k == 0:
                        pe.wait_ge(y0_ready, i + 1)
                        pe.wait_ge(y1_ready, i + 1)
                    if k == 4:
                        pe.wait_ge(gathered, i * 16 + 32)
                        transpose_x()
                    w = down_tile(k // 4)
                    for half in range(2):
                        last = nc.tensor.matmul(pv_bank[half][0:BLK, :], actT[:, k, :],
                                                w[:, k % 4, half * 512:half * 512 + 512],
                                                start=(k == 0), stop=(k == KD - 1))
                    if k == 3:
                        last.then_inc(half_done, 1)
                last.then_inc(down_done, 1)


_INS = ["x", "attn_norm_g", "w_in", "b_forget", "fox_out_g", "sb_out_g", "w_out", "ffn_norm_g", "w_router", "b_router",
        "w_gate_up", "b_gate_up", "w_down", "b_down", "final_norm_g"]


def kernel(**inputs):
    import numpy as _np
    import concourse.bacc as _bacc
    from concourse import mybir as _mybir
    from concourse.bass_utils import run_bass_kernel_spmd as _run

    nc = _bacc.Bacc("TRN2", target_bir_lowering=False, num_devices=1)
    arrays, args = {}, []
    for name in _INS:
        a = _np.ascontiguousarray(inputs[name])
        arrays[f"in_{name}_dram"] = a
        args.append(nc.dram_tensor(f"in_{name}_dram", a.shape, _mybir.dt.from_np(a.dtype), kind="ExternalInput").ap())
    args.append(nc.dram_tensor("out_0_dram", (1, SEQ, D), _mybir.dt.float32, kind="ExternalOutput").ap())
    hybrid_layer(nc, *args)
    r = _run(nc, [arrays], core_ids=[0])
    return r.results[0]["out_0_dram"]
```

```python
from contextlib import ExitStack

import concourse.bass as bass
from concourse import mybir

P = 128
D = 1024
SEQ = 512
NT = SEQ // P
KD = D // P
HEADS = 8
DH = 64
GW = HEADS * DH
NE = 32
TOPK = 4
FF = 1024
BLK = 104
FEW = 64
LIMIT = 7.0
ALPHA = 1.702
EPS = 1e-5
SCALE = 1.0 / DH ** 0.5

PIECE = 4096
SLOTS = 6
MIX_SLOTS = 4
MIX_PIECES = 8
EXTRA_MAX = SEQ * TOPK // BLK
MAXBLK = -(-SEQ // BLK)
NX = EXTRA_MAX + 2
NI = NE + NX
FAR = 4096.0
NEG = -1e30

ALU = mybir.AluOpType
ACT = mybir.ActivationFunctionType
AX = mybir.AxisListType
F32 = mybir.dt.float32
BF16 = mybir.dt.bfloat16
I32 = mybir.dt.int32
U32 = mybir.dt.uint32


def hybrid_layer(nc, x, attn_norm_g, w_in, b_forget, fox_out_g, sb_out_g, w_out, ffn_norm_g,
                 w_router, b_router, w_gate_up, b_gate_up, w_down, b_down, final_norm_g, out):
    ctx = ExitStack()
    with ctx:
        def sb(name, shape, dt=F32):
            return ctx.enter_context(nc.sbuf_tensor(name, shape, dt))

        def sem(name):
            return ctx.enter_context(nc.semaphore(name))

        h2_rows = nc.dram_tensor("h2_rows", [SEQ + P, D], F32, kind="Internal").ap()
        acc_rows = nc.dram_tensor("acc_rows", [SEQ + P, D], F32, kind="Internal").ap()
        negc_rows = nc.dram_tensor("negc_rows", [HEADS, SEQ], F32, kind="Internal").ap()

        ring = sb("ring", [P, SLOTS, PIECE])
        xres = sb("xres", [P, NT, D])
        rows_buf = sb("rows_buf", [P, NT * D])
        cols_buf = sb("cols_buf", [P, NT * D])
        big = sb("big", [P, 12288])

        def part(base, *dims):
            n = 1
            for d in dims:
                n *= d
            v = base
            if len(dims) == 2:
                return v.rearrange("p (a b) -> p a b", b=dims[1])
            if len(dims) == 3:
                return v.rearrange("p (a b c) -> p a b c", b=dims[1], c=dims[2])
            return v

        rows = part(rows_buf[:], NT, D)
        yT = part(rows_buf[:], KD, SEQ)
        bd_tmp = part(rows_buf[:], NT, D)
        colsT = part(cols_buf[:], KD, SEQ)
        h2 = part(cols_buf[:], NT, D)
        qk = part(big[:, 0:8192], 16, SEQ)
        v_sb = part(big[:, 8192:12288], NT, 2 * GW)
        xg_f = part(big[0:HEADS, 4096:4096 + 4 * SEQ], 4, SEQ)
        bgu_rows = big[0:NE, 8192:8192 + 2 * FF]
        negc = part(ring[:, 4, :], HEADS, SEQ)
        wk = part(ring[:, 5, :], 8, SEQ)
        zrow = ring[:, 5, 0:D]

        h2T = part(big[:, 0:4096], KD, SEQ)
        onehot = part(big[:, 4096:4608], NT, TOPK, NE)
        onehot_g = part(big[:, 4608:5120], NT, TOPK, NE)
        gT = big[0:NE, 5120:5632]
        bdown_sb = big[0:NE, 5632:6656]
        itemcmp = part(big[:, 6656:6656 + NX * NE], NX, NE)
        itemcmp2 = part(big[:, 7424:7424 + NX * NE], NX, NE)
        xg = big[0:BLK, 8192:9216]
        xgT = part(big[:, 9216:9216 + KD * BLK], KD, BLK)
        actT = part(big[:, 10240:10240 + KD * BLK], KD, BLK)
        ysb = big[0:BLK, 11264:12288]
        gtile = [part(big[:, 256 * j:256 * j + 2 * BLK], 2, BLK) for j in range(2)]
        utile = [part(big[:, 512 + 256 * j:512 + 256 * j + 2 * BLK], 2, BLK) for j in range(2)]
        stile = [part(big[:, 1024 + 256 * j:1024 + 256 * j + 2 * BLK], 2, BLK) for j in range(2)]
        fing = big[:, 4096:4096 + D]
        logits = part(big[:, 11264:11392], NT, NE)
        maskf = part(big[:, 11392:11520], NT, NE)
        w_r = part(big[:, 11520:11776], KD, NE)
        sel = part(big[:, 2048:2048 + NT * BLK], NT, BLK)

        ident = sb("ident", [P, P])
        identb = sb("identb", [P, P], BF16)
        mask_causal = sb("mask_causal", [P, P], BF16)
        mask_strict = sb("mask_strict", [P, P], BF16)
        before = sb("before", [P, P], BF16)
        ones = sb("ones", [P, P], BF16)
        g_attn = sb("g_attn", [P, KD])
        g_mix = sb("g_mix", [P, KD])
        g_ffn = sb("g_ffn", [P, KD])
        w_f = sb("w_f", [P, KD, HEADS])
        bf_c = sb("bf_c", [HEADS, 1])
        br_b = sb("br_b", [P, NE])
        bgu = sb("bgu", [P, NE, 16])
        ssq = sb("ssq", [P, 16])
        rstd = sb("rstd", [P, 16])
        msq = sb("msq", [P, 16])
        sq = sb("sq", [P, 2, SEQ])
        sqsum = sb("sqsum", [P, SEQ])
        zf = xg_f[:, 0, :]
        lf = xg_f[:, 1, :]
        negc_sb = xg_f[:, 2, :]
        nmax = sb("nmax", [P, 32])
        rsum = sb("rsum", [P, 32])
        rinv = sb("rinv", [P, 32])
        top8 = sb("top8", [P, NT, 8])
        topi = sb("topi", [P, NT, 8], U32)
        topf = sb("topf", [P, NT, 8])
        gexp = sb("gexp", [P, NT, TOPK])
        gsum = sb("gsum", [P, NT])
        ginv = sb("ginv", [P, NT])
        maskb = sb("maskb", [P, NT, NE], BF16)
        gate_et = sb("gate_et", [P, NE * NT])
        rank_et = sb("rank_et", [P, NE * NT])
        counts = sb("counts", [P, NE])
        extra = sb("extra", [P, NE])
        onesrow = sb("onesrow", [P, NE])
        onescol = sb("onescol", [P, 2])
        cumx = sb("cumx", [P, NE])
        iota = sb("iota", [P, P])
        padrow = sb("padrow", [P, 1])
        item_e = sb("item_e", [1, NI], I32)
        item_f = sb("item_f", [P, NI])
        item_few = sb("item_few", [1, NI], I32)
        item_b = sb("item_b", [P, NI])
        n_items_sb = sb("n_items_sb", [1, 1], I32)
        cxj = sb("cxj", [P, NX])
        rel = sb("rel", [P, NT])
        info = sb("info", [P, NT, 4])
        biasc = sb("biasc", [P, 16])
        pausing = sb("pausing", [1, 2])
        padsel = sb("padsel", [BLK, 1])
        idx_next = sb("idx_next", [BLK, 1], I32)
        idx_now = sb("idx_now", [BLK, 1], I32)
        gate_next = sb("gate_next", [BLK, 1])
        gate_now = sb("gate_now", [BLK, 1])

        bank = [ctx.enter_context(nc.psum_tensor(f"bank{i}", [P, 512], F32)) for i in range(8)]
        sc_bank, pt_bank, pv_bank, pj_bank = bank[0:2], bank[2:4], bank[4:6], bank[6:8]

        landed = [sem(f"landed{s}") for s in range(SLOTS)]
        x_in = [sem(f"x_in{t}") for t in range(NT)]
        g_in = sem("g_in")
        f_in = sem("f_in")
        bgu_in = sem("bgu_in")
        r_in = sem("r_in")
        bdown_in = sem("bdown_in")
        fing_in = sem("fing_in")
        pads_out = sem("pads_out")
        negc_out = sem("negc_out")
        negc_in = sem("negc_in")
        h2_out = sem("h2_out")
        acc_out = sem("acc_out")
        consts = sem("consts")
        zero_ok = sem("zero_ok")
        dstep = sem("dstep")
        astep = sem("astep")
        pstep = sem("pstep")
        xn_ready = sem("xn_ready")
        ssx = sem("ssx")
        tr_done = sem("tr_done")
        tr_used_a = sem("tr_used_a")
        tr_used_v = sem("tr_used_v")
        bgu_done = sem("bgu_done")
        bgu_read = sem("bgu_read")
        f_done = sem("f_done")
        zf_ready = sem("zf_ready")
        lf_abs = sem("lf_abs")
        negc_ready = sem("negc_ready")
        proj_done = sem("proj_done")
        proj_read = sem("proj_read")
        score_done = sem("score_done")
        softln = sem("softln")
        arg_ready = sem("arg_ready")
        prob_ready = sem("prob_ready")
        probT_done = sem("probT_done")
        probT_v = sem("probT_v")
        probT_a = sem("probT_a")
        pv_done = sem("pv_done")
        y_ready = sem("y_ready")
        scaled = sem("scaled")
        sq_ready = sem("sq_ready")
        sq_summed = sem("sq_summed")
        ssy_done = sem("ssy_done")
        rstdy = sem("rstdy")
        bd_copied = sem("bd_copied")
        op_done = sem("op_done")
        x1_ready = sem("x1_ready")
        ss1 = sem("ss1")
        h2_ready = sem("h2_ready")
        h2t_done = sem("h2t_done")
        h2t_read = sem("h2t_read")
        rt_done = sem("rt_done")
        gl_ready = sem("gl_ready")
        mask_ready = sem("mask_ready")
        rank_done = sem("rank_done")
        gate_ready = sem("gate_ready")
        gt_done = sem("gt_done")
        gt_read = sem("gt_read")
        bd_done = sem("bd_done")
        acc_ready = sem("acc_ready")
        items_ready = sem("items_ready")
        sel_ready = sem("sel_ready")
        idx_done = sem("idx_done")
        idx_ready = sem("idx_ready")
        gathered = sem("gathered")
        xt_done = sem("xt_done")
        xt_ready = sem("xt_ready")
        gu_done = sem("gu_done")
        gu_used = sem("gu_used")
        g_ready = sem("g_ready")
        s_ready = sem("s_ready")
        act_ready = sem("act_ready")
        half_done = sem("half_done")
        down_done = sem("down_done")
        bias_ready = sem("bias_ready")
        rel_ready = sem("rel_ready")
        u_step = sem("u_step")
        now_ready = sem("now_ready")
        pad_step = sem("pad_step")
        paused = sem("paused")
        rt_read = sem("rt_read")
        msq_ready = sem("msq_ready")
        root_ready = sem("root_ready")
        y0_ready = sem("y0_ready")
        y1_ready = sem("y1_ready")
        scattered = sem("scattered")
        fin_in = sem("fin_in")
        ssf = sem("ssf")
        fin_ready = sem("fin_ready")
        stored = sem("stored")

        OFF_F = 3 * GW
        OFF_B = OFF_F + HEADS
        mix_cols = [OFF_B, OFF_B + GW, OFF_B + 2 * GW, 0, GW, 2 * GW]

        def mix_source(n):
            if n < 6:
                return w_in[:, mix_cols[n]:mix_cols[n] + GW].rearrange("(k p) c -> p k c", p=P)
            r = GW if n == 6 else 0
            return w_out[r:r + GW, :].rearrange("(k p) c -> p k c", p=P)

        def mix_tile(n):
            return part(ring[:, n % MIX_SLOTS, :], *((KD, 512) if n < 6 else (4, D)))

        def gu_tile(q):
            return part(ring[:, q, :], KD, 512)

        def down_tile(h):
            return part(ring[:, 4 + h, :], 4, D)

        NU = 2 * HEADS * NT
        NPAIR = HEADS

        def tile_of(u):
            r = u % 32
            return u // 32, 2 * (r // 8) + r % 2, (r % 8) // 2

        def prob_tile(u):
            return wk[:, 4 + u % 2, :] if u < 32 else wk[:, u % 4, :]

        block = ctx.enter_context(nc.Block())

        @block.sync
        def _(sp):
            xv = x[0].rearrange("(t p) d -> p t d", p=P)
            for t in range(NT):
                sp.dma_start(xres[:, t, :], xv[:, t, :]).then_inc(x_in[t], 16)
            for n in range(MIX_PIECES):
                if n >= MIX_SLOTS:
                    sp.wait_ge(proj_done, 4 * (n - MIX_SLOTS + 1))
                sp.dma_start(mix_tile(n), mix_source(n)).then_inc(landed[n % MIX_SLOTS], 16)

            def load_item_piece(e, j):
                if j < 4:
                    src = w_gate_up[e, :, j * 512:(j + 1) * 512].rearrange("(k p) c -> p k c", p=P)
                    dst = gu_tile(j)
                else:
                    src = w_down[e, (j - 4) * 512:(j - 3) * 512, :].rearrange("(k p) c -> p k c", p=P)
                    dst = down_tile(j - 4)
                sp.dma_start(dst, src).then_inc(landed[j], 16)

            for j in (0, 1):
                sp.wait_ge(proj_done, 4 * (4 + j + 1))
                load_item_piece(0, j)
            sp.wait_ge(y_ready, NPAIR)
            for j in (4, 5):
                load_item_piece(0, j)
            for j in (2, 3):
                sp.wait_ge(op_done, 2 * NT * (j - 1))
                load_item_piece(0, j)
            sp.wait_ge(items_ready, 1)
            n_items = sp.value_load(n_items_sb[0:1, 0:1], min_val=NE, max_val=NE + EXTRA_MAX)
            with sp.Fori(1, n_items) as i:
                e = sp.value_load(item_e[0:1, bass.ds(i, 1)], min_val=0, max_val=NE - 1)
                for j in range(6):
                    if j < 4:
                        sp.wait_ge(gu_done, i * 4 + (j - 3))
                    elif j == 4:
                        sp.wait_ge(half_done, i)
                    else:
                        sp.wait_ge(down_done, i)
                    if j < 4:
                        src = w_gate_up[bass.ds(e, 1), :, j * 512:(j + 1) * 512].rearrange(
                            "a (k p) c -> p (a k) c", p=P)
                        sp.dma_start(gu_tile(j), src).then_inc(landed[j], 16)
                    else:
                        src = w_down[bass.ds(e, 1), (j - 4) * 512:(j - 3) * 512, :].rearrange(
                            "a (k p) c -> p (a k) c", p=P)
                        sp.dma_start(down_tile(j - 4), src).then_inc(landed[j], 16)

        @block.gpsimd
        def _(pool):
            chain = [0]

            def link(ins):
                chain[0] += 1
                ins.then_inc(pstep, 1)
                pool.wait_ge(pstep, chain[0])

            def tri(dst, keep, fill, op, step, mult, width=P):
                link(nc.gpsimd.memset(dst, keep))
                return nc.gpsimd.affine_select(out=dst, in_=dst, compare_op=op, fill=fill, base=0,
                                               pattern=[[step, width]], channel_multiplier=mult)

            tri(ident[:], 0.0, 1.0, ALU.not_equal, -1, 1).then_inc(consts, 1)
            nc.gpsimd.memset(zrow, 0.0).then_inc(zero_ok, 1)
            nc.gpsimd.memset(onescol[:], 1.0).then_inc(consts, 1)
            tri(identb[:], 0.0, 1.0, ALU.not_equal, -1, 1).then_inc(consts, 1)
            tri(mask_strict[:], 0.0, NEG, ALU.is_gt, -1, 1).then_inc(consts, 1)
            tri(mask_causal[:], 0.0, NEG, ALU.is_ge, -1, 1).then_inc(consts, 1)
            tri(before[:], 1.0, 0.0, ALU.is_gt, 1, -1).then_inc(consts, 1)
            nc.gpsimd.memset(ones[:], 1.0).then_inc(consts, 1)
            nc.gpsimd.memset(onesrow[:], 1.0).then_inc(consts, 1)
            link(nc.gpsimd.memset(info[:], 1.0))
            nc.gpsimd.iota(iota[:], [[1, P]], base=0, channel_multiplier=0,
                           allow_small_or_imprecise_dtypes=True).then_inc(consts, 1)
            nc.gpsimd.iota(padrow[:], [[1, 1]], base=SEQ, channel_multiplier=1,
                           allow_small_or_imprecise_dtypes=True).then_inc(consts, 1)
            nc.gpsimd.iota(info[:, :, 0], [[P, NT]], base=0, channel_multiplier=1,
                           allow_small_or_imprecise_dtypes=True).then_inc(consts, 1)
            nc.gpsimd.iota(item_f[:], [[1, NI]], base=0, channel_multiplier=0,
                           allow_small_or_imprecise_dtypes=True).then_inc(consts, 1)
            nc.gpsimd.memset(item_few[:], 0)
            nc.gpsimd.memset(item_b[:], -FAR).then_inc(consts, 1)
            nc.gpsimd.memset(pausing[:], 0.0).then_inc(paused, 1)
            pool.wait_ge(zero_ok, 1)
            pool.dma_start(acc_rows[SEQ:SEQ + P, :], zrow).then_inc(scattered, 16)

            for c in range(NPAIR):
                pool.wait_ge(sq_ready, c + 1)
                if c == 4:
                    pool.wait_ge(ssy_done, 1)
                if c % 4 == 0:
                    ins = nc.gpsimd.tensor_copy(sqsum[:], sq[:, c % 2, :])
                else:
                    ins = nc.gpsimd.tensor_tensor(sqsum[:], sqsum[:], sq[:, c % 2, :], ALU.add)
                ins.then_inc(sq_summed, 1)
                pool.wait_ge(sq_summed, c + 1)

            def pause(c):
                nc.gpsimd.tensor_tensor(pausing[:, c:c + 1], onesrow[0:1, 0:1], onesrow[0:1, 0:1], ALU.add
                                        ).then_inc(paused, 1)

            def gather():
                pool.indirect_dma_start(out=xg, out_offset=None, in_=h2_rows,
                                        in_offset=bass.IndirectOffsetOnAxis(ap=idx_next[:, 0:1], axis=0)
                                        ).then_inc(gathered, 16)

            pool.wait_ge(h2_out, 16 * NT)
            pool.wait_ge(pads_out, 16)
            pool.wait_ge(idx_ready, 1)
            gather()
            for m in range(2 * NT):
                t, half = m // 2, m % 2
                pool.wait_ge(bd_copied, m + 1)
                c = slice(half * 512, half * 512 + 512)
                nc.gpsimd.tensor_tensor(xres[:, t, c], xres[:, t, c], bd_tmp[:, t, c], ALU.add).then_inc(acc_ready, 1)
            pool.wait_ge(acc_out, 16 * NT)
            pool.wait_ge(items_ready, 1)
            n_items = pool.value_load(n_items_sb[0:1, 0:1], min_val=NE, max_val=NE + EXTRA_MAX)
            with pool.Fori(0, n_items) as i:
                pool.wait_ge(paused, i * 2 + 1)
                pool.wait_ge(idx_ready, i + 2)
                pool.wait_ge(xt_done, i + 1)
                pause(0)
                gather()
                pool.wait_ge(y0_ready, i + (NT + 1))
                pool.wait_ge(y1_ready, i + 2)
                pool.wait_ge(scattered, i * 16 + 16)
                pause(1)
                pool.indirect_dma_start(out=acc_rows, out_offset=bass.IndirectOffsetOnAxis(ap=idx_now[:, 0:1], axis=0),
                                        in_=ysb, in_offset=None, compute_op=ALU.add).then_inc(scattered, 16)
            pool.wait_ge(scattered, n_items * 16 + 16)

        @block.scalar
        def _(act):
            chain = [0]

            def link(ins):
                chain[0] += 1
                ins.then_inc(astep, 1)
                act.wait_ge(astep, chain[0])

            root_count = [0]

            def root(col, n):
                c = slice(col, col + n)
                root_count[0] += 1
                act.wait_ge(msq_ready, root_count[0])
                link(nc.scalar.activation(msq[:, c], msq[:, c], ACT.Ln))
                nc.scalar.activation(rstd[:, c], msq[:, c], ACT.Exp, scale=0.5).then_inc(root_ready, 1)

            nc.scalar.preload_act_table_set("natural_log_exp_and_others")
            ov = out[0].rearrange("(t p) d -> p t d", p=P)
            with nc.allow_non_contiguous_dma(reason="gains, one per partition"):
                act.dma_start(g_attn[:], attn_norm_g.rearrange("(k p) -> p k", p=P)).then_inc(g_in, 16)
                act.dma_start(g_mix[:, 0:4], fox_out_g.rearrange("(k p) -> p k", p=P)).then_inc(g_in, 16)
                act.dma_start(g_mix[:, 4:8], sb_out_g.rearrange("(k p) -> p k", p=P)).then_inc(g_in, 16)
                act.dma_start(g_ffn[:], ffn_norm_g.rearrange("(k p) -> p k", p=P)).then_inc(g_in, 16)
                act.dma_start(w_f[:], w_in[:, OFF_F:OFF_F + HEADS].rearrange("(k p) c -> p k c", p=P)).then_inc(f_in, 16)
                act.dma_start(bf_c[:], b_forget.rearrange("(h a) -> h a", a=1)).then_inc(f_in, 16)
            act.dma_start(bgu_rows, b_gate_up).then_inc(bgu_in, 16)
            act.dma_start(br_b[:], b_router.rearrange("(a h) -> a h", a=1).to_broadcast([P, NE])).then_inc(r_in, 16)
            act.wait_ge(zero_ok, 1)
            act.dma_start(h2_rows[SEQ:SEQ + P, :], zrow).then_inc(pads_out, 16)

            for t in range(NT):
                act.wait_ge(x_in[t], 16)
                nc.scalar.activation(rows[:, t, :], xres[:, t, :], ACT.Square, accum_out=ssq[:, t:t + 1]).then_inc(ssx, 1)
                root(t, 1)

            act.wait_ge(g_in, 64)
            for k in range(0, KD, 2):
                act.wait_ge(tr_done, k + 1)
                nc.scalar.activation(colsT[:, k, :], pj_bank[0][:, :], ACT.Copy, scale=g_attn[:, k:k + 1]
                                     ).then_inc(tr_used_a, 1)

            def forget():
                act.wait_ge(zf_ready, 1)
                link(nc.scalar.activation(lf, zf, ACT.Abs))
                link(nc.scalar.activation(lf, lf, ACT.Exp, scale=-1.0))
                nc.scalar.activation(lf, lf, ACT.Ln, bias=1.0).then_inc(lf_abs, 1)

            def negc_copy():
                act.wait_ge(negc_ready, 1)
                act.dma_start(negc_rows, negc_sb).then_inc(negc_out, 16)
                act.wait_ge(negc_out, 16)
                src = negc_rows.rearrange("(a h) s -> a (h s)", a=1).to_broadcast([P, HEADS * SEQ])
                act.dma_start(ring[:, 4, :], src).then_inc(negc_in, 16)

            def read_proj(n):
                act.wait_ge(proj_done, n + 1)
                ps = pj_bank[n % 2]
                g, c = n // 4, n % 4
                if g in (2, 5):
                    dst = v_sb[:, c, (GW if g == 2 else 0):(GW if g == 2 else 0) + GW]
                    ins = nc.scalar.copy(dst, ps[:, :])
                else:
                    slot = {0: 0, 1: 4, 3: 8, 4: 12}[g] + c
                    if g in (0, 3):
                        ins = nc.scalar.activation(qk[:, slot, :], ps[:, :], ACT.Copy, scale=SCALE)
                    else:
                        ins = nc.scalar.copy(qk[:, slot, :], ps[:, :])
                ins.then_inc(proj_read, 1)

            def soft(u):
                g, h, t = tile_of(u)
                w = (t + 1) * P
                act.wait_ge(score_done, u + 1)
                if u == 0:
                    act.wait_ge(pads_out, 16)
                    act.wait_ge(scattered, 16)
                if u >= 2:
                    act.wait_ge(arg_ready, u - 1)
                link(nc.scalar.activation(wk[:, u % 2, 0:w], sc_bank[u % 2][:, 0:w], ACT.Abs))
                link(nc.scalar.activation(wk[:, u % 2, 0:w], wk[:, u % 2, 0:w], ACT.Exp, scale=-1.0))
                nc.scalar.activation(wk[:, u % 2, 0:w], wk[:, u % 2, 0:w], ACT.Ln, bias=1.0).then_inc(softln, 1)

            def prob(u):
                g, h, t = tile_of(u)
                w = (t + 1) * P
                act.wait_ge(arg_ready, u + 1)
                p = prob_tile(u)[:, 0:w]
                if g == 0:
                    nc.scalar.activation(p, p, ACT.Exp).then_inc(prob_ready, 1)
                else:
                    c = u - 32
                    nc.scalar.activation(p, p, ACT.Exp, scale=-1.0,
                                         bias=nmax[:, c:c + 1], accum_out=rsum[:, c:c + 1]).then_inc(prob_ready, 1)

            def copy_probT(u):
                g, h, t = tile_of(u)
                w = (t + 1) * P
                act.wait_ge(probT_done, u + 1)
                act.wait_ge(pv_done, u // 2)
                nc.scalar.copy(wk[:, 6 + u % 2, 0:w], pt_bank[u % 2][:, 0:w]).then_inc(probT_a, 1)

            def square(c):
                act.wait_ge(pv_done, 4 * (c + 1))
                if c >= 2:
                    act.wait_ge(sq_summed, c - 1)
                nc.scalar.activation(sq[:, c % 2, :], pv_bank[c % 2][:, :], ACT.Square).then_inc(sq_ready, 1)

            for n in range(8):
                read_proj(n)
            forget()
            for n in range(NU // 2 + 3):
                if n < 16:
                    read_proj(8 + n)
                    soft(2 * n)
                if 1 <= n <= 16:
                    prob(2 * n - 1)
                if n < 16:
                    soft(2 * n + 1)
                    prob(2 * n)
                if n == 1:
                    negc_copy()
                for j in (0, 1):
                    if 16 <= n < NU // 2:
                        prob(2 * n + j)
                    if 32 <= 2 * n - 2 + j < NU:
                        copy_probT(2 * n - 2 + j)
                if n >= 6 and (n - 6) % 4 == 0:
                    square((n - 6) // 4)
                if n == 22:
                    root(4, 4)
            root(8, 4)

            act.wait_ge(y_ready, NPAIR)
            act.dma_start(w_r, w_router.rearrange("(k p) c -> p k c", p=P)).then_inc(r_in, 16)
            act.dma_start(bdown_sb, b_down).then_inc(bdown_in, 16)

            for t in range(NT + 2):
                if t < NT:
                    act.wait_ge(x1_ready, 2 * NT + 2 * (t + 1))
                    nc.scalar.activation(h2[:, t, :], xres[:, t, :], ACT.Square,
                                         accum_out=ssq[:, 12 + t:13 + t]).then_inc(ss1, 1)
                    root(12 + t, 1)
                    act.wait_ge(h2_ready, t + 1)
                    act.dma_start(h2_rows[t * P:(t + 1) * P, :], h2[:, t, :]).then_inc(h2_out, 16)
                if t >= 2:
                    act.wait_ge(gl_ready, t - 1)
                    nc.scalar.activation(gexp[:, t - 2, :], gexp[:, t - 2, :], ACT.Exp).then_inc(y0_ready, 1)

            for m in range(2 * NT):
                t, half = m // 2, m % 2
                act.wait_ge(bd_done, m + 1)
                nc.scalar.copy(bd_tmp[:, t, half * 512:half * 512 + 512], sc_bank[m % 2][:, :]).then_inc(bd_copied, 1)
            for t in range(NT):
                act.wait_ge(acc_ready, 2 * (t + 1))
                act.dma_start(acc_rows[t * P:(t + 1) * P, :], xres[:, t, :]).then_inc(acc_out, 16)

            act.wait_ge(items_ready, 1)
            n_items = act.value_load(n_items_sb[0:1, 0:1], min_val=NE, max_val=NE + EXTRA_MAX)
            with act.Fori(0, n_items) as i:
                for q in range(4):
                    act.wait_ge(g_ready, i * 4 + (q + 1))
                    nc.scalar.activation(stile[q % 2], gtile[q % 2], ACT.Sigmoid, scale=ALPHA).then_inc(s_ready, 1)
                act.wait_ge(down_done, i + 1)
                act.wait_ge(idx_ready, i + 2)
                act.wait_ge(scattered, i * 16 + 16)
                nc.scalar.activation(ysb[:, 0:512], pv_bank[0][0:BLK, :], ACT.Copy, scale=gate_now[:, 0:1]
                                     ).then_inc(y0_ready, 1)

            nc.scalar.preload_act_table_set("natural_log_exp_and_others")
            act.dma_start(fing, final_norm_g.rearrange("(a d) -> a d", a=1).to_broadcast([P, D])).then_inc(fing_in, 16)
            act.wait_ge(scattered, n_items * 16 + 16)
            for t in range(NT):
                act.dma_start(xres[:, t, :], acc_rows[t * P:(t + 1) * P, :]).then_inc(x_in[t], 16)
            for t in range(NT):
                act.wait_ge(x_in[t], 32)
                nc.scalar.activation(rows[:, t, :], xres[:, t, :], ACT.Square, accum_out=ssq[:, t:t + 1]).then_inc(ssf, 1)
                root(t, 1)
            for t in range(NT):
                act.wait_ge(fin_ready, t + 1)
                act.dma_start(ov[:, t, :], rows[:, t, :]).then_inc(stored, 16)
            act.wait_ge(stored, 16 * NT)

        @block.vector
        def _(dve):
            chain = [0]

            def link(ins):
                chain[0] += 1
                ins.then_inc(dstep, 1)
                dve.wait_ge(dstep, chain[0])

            rms_count = [0]

            def rms(col, n, width, src=None):
                c = slice(col, col + n)
                nc.vector.tensor_scalar(msq[:, c], ssq[:, c] if src is None else src, 1.0 / width, EPS, ALU.mult, ALU.add).then_inc(msq_ready, 1)
                rms_count[0] += 1
                dve.wait_ge(root_ready, rms_count[0])
                link(nc.vector.reciprocal(rstd[:, c], rstd[:, c]))

            for t in range(NT):
                dve.wait_ge(ssx, t + 1)
                rms(t, 1, D)
                nc.vector.tensor_scalar(rows[:, t, :], xres[:, t, :], rstd[:, t:t + 1], None, ALU.mult
                                        ).then_inc(xn_ready, 1)
            dve.wait_ge(g_in, 64)
            for k in range(1, KD, 2):
                dve.wait_ge(tr_done, k + 1)
                nc.vector.tensor_scalar(colsT[:, k, :], pj_bank[1][:, :], g_attn[:, k:k + 1], None, ALU.mult
                                        ).then_inc(tr_used_v, 1)
            def read_bgu():
                dve.wait_ge(bgu_done, 1)
                nc.vector.tensor_copy(bgu[:].rearrange("p e c -> p c e"),
                                      pt_bank[0][:, :].rearrange("p (c e) -> p c e", e=NE)).then_inc(bgu_read, 1)

            def forget_z():
                dve.wait_ge(f_in, 32)
                dve.wait_ge(f_done, 1)
                nc.vector.tensor_scalar(zf, pt_bank[1][0:HEADS, :], bf_c[:, 0:1], -1.0, ALU.add, ALU.mult
                                        ).then_inc(zf_ready, 1)

            def forget_sum():
                dve.wait_ge(lf_abs, 1)
                link(nc.vector.scalar_tensor_tensor(out=lf, in0=zf, scalar=0.0, in1=lf, op0=ALU.max, op1=ALU.add))
                dve.wait_ge(consts, 13)
                nc.vector.tensor_tensor_scan(out=negc_sb, data0=onesrow[0:HEADS, 0:1].to_broadcast([HEADS, SEQ]),
                                             data1=lf, initial=0.0, op0=ALU.mult, op1=ALU.add).then_inc(negc_ready, 1)

            def arg(u):
                g, h, t = tile_of(u)
                w = (t + 1) * P
                if g == 0:
                    dve.wait_ge(softln, u + 1)
                    z = sc_bank[u % 2][:, 0:w]
                    link(nc.vector.scalar_tensor_tensor(out=wk[:, 2, 0:w], in0=z, scalar=0.0, in1=wk[:, u % 2, 0:w],
                                                        op0=ALU.max, op1=ALU.add))
                    link(nc.vector.tensor_tensor_scan(out=wk[:, 3, w - 1::-1], data0=onesrow[:, 0:1].to_broadcast([P, w]),
                                                      data1=wk[:, 2, w - 1::-1], initial=0.0,
                                                      op0=ALU.mult, op1=ALU.add))
                    if u >= 2:
                        dve.wait_ge(probT_done, u - 1)
                    nc.vector.tensor_tensor(wk[:, 4 + u % 2, 0:w], z, wk[:, 3, 0:w], ALU.subtract).then_inc(arg_ready, 1)
                else:
                    c = u - 32
                    dve.wait_ge(score_done, u + 1)
                    if c == 0:
                        dve.wait_ge(negc_in, 16)
                    if c >= 4:
                        dve.wait_ge(probT_done, u - 3)
                    nc.vector.tensor_tensor_reduce(out=prob_tile(u)[:, 0:w], in0=sc_bank[u % 2][:, 0:w],
                                                   in1=negc[:, h, 0:w], scale=-1.0, scalar=3e38, op0=ALU.add,
                                                   op1=ALU.min, accum_out=nmax[:, c:c + 1]).then_inc(arg_ready, 1)

            def copy_probT(u):
                g, h, t = tile_of(u)
                w = (t + 1) * P
                dve.wait_ge(probT_done, u + 1)
                if u >= 2:
                    dve.wait_ge(pv_done, u // 2)
                nc.vector.tensor_copy(wk[:, 6 + u % 2, 0:w], pt_bank[u % 2][:, 0:w]).then_inc(probT_v, 1)

            def scale_prob(u):
                g, h, t = tile_of(u)
                c, w = u - 32, (t + 1) * P
                dve.wait_ge(prob_ready, u + 1)
                link(nc.vector.reciprocal(rinv[:, c:c + 1], rsum[:, c:c + 1]))
                nc.vector.tensor_scalar(prob_tile(u)[:, 0:w], prob_tile(u)[:, 0:w], rinv[:, c:c + 1], None, ALU.mult
                                        ).then_inc(scaled, 1)

            def read_y(c):
                dve.wait_ge(sq_ready, c + 1)
                k = (4 if c < 4 else 0) + c % 4
                nc.vector.tensor_scalar(yT[:, k, :], pv_bank[c % 2][:, :], g_mix[:, k:k + 1], None, ALU.mult
                                        ).then_inc(y_ready, 1)

            def norm_y(g):
                dve.wait_ge(ssy_done, g + 1)
                rms(4 + 4 * g, 4, GW, pt_ssq)

            def read_op(m):
                g, t, half = m // 8, (m % 8) // 2, m % 2
                dve.wait_ge(op_done, m + 1)
                c = slice(half * 512, half * 512 + 512)
                nc.vector.scalar_tensor_tensor(out=xres[:, t, c], in0=pj_bank[m % 2][:, :],
                                               scalar=rstd[:, 4 + 4 * g + t:5 + 4 * g + t], in1=xres[:, t, c],
                                               op0=ALU.mult, op1=ALU.add).then_inc(x1_ready, 1)

            pt_ssq = pj_bank[0][:, 0:8].rearrange("p (t a) -> p t a", a=2)[:, :, 0]
            dve.wait_ge(tr_done, KD)
            for n in range(NU // 2 + 3):
                if n == 0:
                    read_bgu()
                    forget_z()
                for u in (2 * n - 2, 2 * n - 1):
                    if 32 <= u < NU:
                        scale_prob(u)
                for u in (2 * n, 2 * n + 1):
                    if u < NU:
                        arg(u)
                if n == 0:
                    forget_sum()
                for u in (2 * n - 2, 2 * n - 1):
                    if 0 <= u < 32:
                        copy_probT(u)
                if n >= 6 and (n - 6) % 4 == 0:
                    read_y((n - 6) // 4)
                if n == 22:
                    norm_y(0)
                if 24 <= n < 32:
                    read_op(n - 24)
            norm_y(1)

            def norm_1(t):
                dve.wait_ge(ss1, t + 1)
                rms(12 + t, 1, D)
                nc.vector.tensor_scalar(h2[:, t, :], xres[:, t, :], rstd[:, 12 + t:13 + t], None, ALU.mult
                                        ).then_inc(h2_ready, 1)

            def read_h2t(t):
                for hf in range(2):
                    dve.wait_ge(h2t_done, 2 * t + hf + 1)
                    nc.vector.tensor_tensor(h2T[:, 4 * hf:4 * hf + 4, t * P:(t + 1) * P],
                                            pt_bank[hf][:, :].rearrange("p (k c) -> p k c", c=P),
                                            g_ffn[:, 4 * hf:4 * hf + 4].rearrange("p (k a) -> p k a", a=1)
                                            .to_broadcast([P, 4, P]), ALU.mult).then_inc(h2t_read, 1)

            def route(t):
                dve.wait_ge(r_in, 32)
                dve.wait_ge(rt_done, t + 1)
                nc.vector.scalar_tensor_tensor(out=logits[:, t, :], in0=sc_bank[t % 2][:, 0:NE],
                                               scalar=rstd[:, 12 + t:13 + t], in1=br_b[:], op0=ALU.mult, op1=ALU.add
                                               ).then_inc(rt_read, 1)
                dve.wait_ge(rt_read, t + 1)
                link(nc.vector.max(top8[:, t, :], logits[:, t, :]))
                nc.vector.tensor_scalar(gexp[:, t, :], top8[:, t, 0:TOPK], top8[:, t, 0:1], None, ALU.subtract
                                        ).then_inc(gl_ready, 1)
                link(nc.vector.max_index(topi[:, t, :], top8[:, t, :], logits[:, t, :]))
                link(nc.vector.tensor_copy(topf[:, t, :], topi[:, t, :]))
                link(nc.vector.tensor_tensor(
                    onehot[:, t], iota[:, 0:NE].rearrange("p (b e) -> p b e", b=1).to_broadcast([P, TOPK, NE]),
                    topf[:, t, 0:TOPK].rearrange("p (k a) -> p k a", a=1).to_broadcast([P, TOPK, NE]), ALU.is_equal))
                link(nc.vector.tensor_reduce(maskf[:, t, :], onehot[:, t].rearrange("p k e -> p e k"), AX.X, ALU.add))
                nc.vector.tensor_copy(maskb[:, t, :], maskf[:, t, :]).then_inc(mask_ready, 1)

            def gate(t):
                dve.wait_ge(y0_ready, t + 1)
                link(nc.vector.tensor_reduce(gsum[:, t:t + 1], gexp[:, t, :], AX.X, ALU.add))
                link(nc.vector.reciprocal(ginv[:, t:t + 1], gsum[:, t:t + 1]))
                link(nc.vector.tensor_scalar(gexp[:, t, :], gexp[:, t, :], ginv[:, t:t + 1], None, ALU.mult))
                link(nc.vector.tensor_tensor(onehot_g[:, t], onehot[:, t],
                                             gexp[:, t, :].rearrange("p (k a) -> p k a", a=1)
                                             .to_broadcast([P, TOPK, NE]), ALU.mult))
                nc.vector.tensor_reduce(gate_et[:].rearrange("p (e t) -> p t e", t=NT)[:, t, :],
                                        onehot_g[:, t].rearrange("p k e -> p e k"), AX.X, ALU.add).then_inc(gate_ready, 1)

            for t in range(NT + 2):
                if t < NT:
                    read_op(8 + 2 * t)
                    read_op(9 + 2 * t)
                if 1 <= t <= NT:
                    read_h2t(t - 1)
                if t < NT:
                    norm_1(t)
                if t >= 2:
                    route(t - 2)
                    gate(t - 2)
            dve.wait_ge(rank_done, 1)
            link(nc.vector.scalar_tensor_tensor(
                out=rank_et[:].rearrange("p (e t) -> p t e", t=NT), in0=maskf, scalar=-FAR,
                in1=pj_bank[0][:, 0:NT * NE].rearrange("p (t e) -> p t e", e=NE), op0=ALU.mult, op1=ALU.add))
            link(nc.vector.tensor_copy(counts[:], pj_bank[0][:, NT * NE:(NT + 1) * NE]))
            link(nc.vector.tensor_scalar(rel[:], rank_et[:, 0:NT], item_b[:, 0:1], None, ALU.subtract))
            nc.vector.tensor_copy(info[:, :, 2], gate_et[:, 0:NT]).then_inc(gu_used, 2)
            for t in range(NT):
                ins = nc.vector.tensor_scalar(sel[:, t, :], iota[:, 0:BLK], rel[:, t:t + 1], None, ALU.is_equal)
            ins.then_inc(sel_ready, 1)

            def read_idx():
                ps = pj_bank[0]
                nc.vector.tensor_copy(gate_next[:], ps[0:BLK, 2:3])
                link(nc.vector.tensor_scalar(padsel[:], ps[0:BLK, 1:2], 0.0, padrow[0:BLK, 0:1], ALU.is_equal, ALU.mult))
                nc.vector.tensor_tensor(idx_next[:], padsel[:], ps[0:BLK, 0:1], ALU.add).then_inc(idx_ready, 1)

            def read_xt():
                for hf in range(2):
                    ins = nc.vector.tensor_tensor(
                        xgT[:, 4 * hf:4 * hf + 4, :], pt_bank[hf][:, 0:4 * BLK].rearrange("p (k c) -> p k c", c=BLK),
                        g_ffn[:, 4 * hf:4 * hf + 4].rearrange("p (k a) -> p k a", a=1).to_broadcast([P, 4, BLK]),
                        ALU.mult)
                ins.then_inc(xt_ready, 1)

            dve.wait_ge(idx_done, 1)
            read_idx()
            dve.wait_ge(gt_done, 1)
            nc.vector.tensor_copy(gT, pt_bank[0][0:NE, :]).then_inc(gt_read, 1)
            nc.vector.tensor_scalar(item_few[:, 0:NE], counts[0:1, :], float(FEW), None, ALU.is_le)
            link(nc.vector.tensor_scalar(extra[:], counts[:], float(BLK), None, ALU.is_gt))
            for b in range(2, MAXBLK):
                link(nc.vector.scalar_tensor_tensor(out=extra[:], in0=counts[:], scalar=float(b * BLK), in1=extra[:],
                                                    op0=ALU.is_gt, op1=ALU.add))
            link(nc.vector.tensor_tensor_scan(out=cumx[:], data0=onesrow[:], data1=extra[:], initial=0.0,
                                              op0=ALU.mult, op1=ALU.add))
            link(nc.vector.tensor_scalar(n_items_sb[:], cumx[0:1, NE - 1:NE], float(NE), None, ALU.add))
            cum_b = cumx[:].rearrange("p (a e) -> p a e", a=1).to_broadcast([P, NX, NE])
            ext_b = extra[:].rearrange("p (a e) -> p a e", a=1).to_broadcast([P, NX, NE])
            j_b = iota[:, 0:NX].rearrange("p (j a) -> p j a", a=1).to_broadcast([P, NX, NE])
            link(nc.vector.tensor_tensor(itemcmp, cum_b, j_b, ALU.is_le))
            link(nc.vector.tensor_tensor(itemcmp2, itemcmp, ext_b, ALU.mult))
            link(nc.vector.tensor_reduce(item_f[:, NE:NI], itemcmp, AX.X, ALU.add))
            link(nc.vector.tensor_scalar(item_f[:, NE:NI], item_f[:, NE:NI], float(NE - 1), None, ALU.min))
            link(nc.vector.tensor_reduce(cxj[:], itemcmp2, AX.X, ALU.add))
            link(nc.vector.tensor_tensor(cxj[:], iota[:, 0:NX], cxj[:], ALU.subtract))
            link(nc.vector.tensor_scalar(item_b[:, NE:NI], cxj[:], float(BLK), float(BLK) - FAR, ALU.mult, ALU.add))
            nc.vector.tensor_copy(item_e[:], item_f[0:1, :]).then_inc(items_ready, 1)
            dve.wait_ge(items_ready, 1)

            dve.wait_ge(xt_done, 1)
            read_xt()
            nc.vector.memset(biasc[:], 0.0).then_inc(y1_ready, 1)
            dve.wait_ge(y1_ready, 1)

            n_items = dve.value_load(n_items_sb[0:1, 0:1], min_val=NE, max_val=NE + EXTRA_MAX)
            with dve.Fori(0, n_items) as i:
                e_now = dve.value_load(item_e[0:1, bass.ds(i, 1)], min_val=0, max_val=NE - 1)
                e_next = dve.value_load(item_e[0:1, bass.ds(i + 1, 1)], min_val=0, max_val=NE - 1)
                nc.vector.tensor_copy(biasc[:], bgu[:].rearrange("p e c -> p (e c)")[:, bass.ds(e_now * 16, 16)]
                                      ).then_inc(bias_ready, 1)
                dve.wait_ge(idx_done, i + 1)
                nc.vector.tensor_scalar(rel[:], rank_et[:, bass.ds(e_next * NT, NT)], item_b[:, bass.ds(i + 1, 1)],
                                        None, ALU.subtract).then_inc(rel_ready, 1)
                nc.vector.tensor_copy(info[:, :, 2], gate_et[:, bass.ds(e_next * NT, NT)])
                dve.wait_ge(rel_ready, i + 1)
                for t in range(NT):
                    ins = nc.vector.tensor_scalar(sel[:, t, :], iota[:, 0:BLK], rel[:, t:t + 1], None, ALU.is_equal)
                ins.then_inc(sel_ready, 1)
                dve.wait_ge(bias_ready, i + 1)
                for q in range(4):
                    gt, ut, st, ps = gtile[q % 2], utile[q % 2], stile[q % 2], sc_bank[q % 2]
                    dve.wait_ge(gu_done, i * 4 + (q + 1))
                    for jj in range(2):
                        c = 4 * q + 2 * jj
                        gi = nc.vector.tensor_scalar(gt[:, jj, :], ps[:, (2 * jj) * BLK:(2 * jj + 1) * BLK],
                                                     biasc[:, c:c + 1], LIMIT, ALU.add, ALU.min)
                    gi.then_inc(g_ready, 1)
                    for jj in range(2):
                        c = 4 * q + 2 * jj + 1
                        ui = nc.vector.tensor_scalar(ut[:, jj, :], ps[:, (2 * jj + 1) * BLK:(2 * jj + 2) * BLK],
                                                     biasc[:, c:c + 1], LIMIT, ALU.add, ALU.min)
                    ui.then_inc(gu_used, 1)
                    dve.wait_ge(gu_used, i * 4 + (q + 3))
                    nc.vector.tensor_scalar(ut, ut, -LIMIT, 1.0, ALU.max, ALU.add).then_inc(u_step, 1)
                    dve.wait_ge(u_step, i * 8 + (2 * q + 1))
                    dve.wait_ge(g_ready, i * 4 + (q + 1))
                    nc.vector.tensor_tensor(ut, gt, ut, ALU.mult).then_inc(u_step, 1)
                    dve.wait_ge(u_step, i * 8 + (2 * q + 2))
                    dve.wait_ge(s_ready, i * 4 + (q + 1))
                    nc.vector.tensor_tensor(actT[:, 2 * q:2 * q + 2, :], ut, st, ALU.mult).then_inc(act_ready, 1)
                    if q == 0:
                        dve.wait_ge(scattered, i * 16 + 16)
                        nc.vector.tensor_copy(gate_now[:], gate_next[:])
                        nc.vector.tensor_copy(idx_now[:], idx_next[:]).then_inc(now_ready, 1)
                        dve.wait_ge(now_ready, i + 1)
                        dve.wait_ge(idx_done, i + 2)
                        ps0 = pj_bank[0]
                        nc.vector.tensor_copy(gate_next[:], ps0[0:BLK, 2:3])
                        nc.vector.tensor_scalar(padsel[:], ps0[0:BLK, 1:2], 0.0, padrow[0:BLK, 0:1], ALU.is_equal,
                                                ALU.mult).then_inc(pad_step, 1)
                        dve.wait_ge(pad_step, i + 1)
                        nc.vector.tensor_tensor(idx_next[:], padsel[:], ps0[0:BLK, 0:1], ALU.add).then_inc(idx_ready, 1)
                dve.wait_ge(xt_done, i + 2)
                read_xt()
                dve.wait_ge(down_done, i + 1)
                few = dve.value_load(item_few[0:1, bass.ds(i, 1)], min_val=0, max_val=1)
                with dve.If(few):
                    nc.vector.tensor_scalar(ysb[0:FEW, 512:D], pv_bank[1][P // 2:P // 2 + FEW, :], gate_now[0:FEW, 0:1], None,
                                            ALU.mult).then_inc(y1_ready, 1)
                with dve.Else():
                    nc.vector.tensor_scalar(ysb[:, 512:D], pv_bank[1][0:BLK, :], gate_now[:, 0:1], None, ALU.mult
                                            ).then_inc(y1_ready, 1)

            for t in range(NT):
                dve.wait_ge(ssf, t + 1)
                rms(t, 1, D)
                dve.wait_ge(fing_in, 16)
                nc.vector.scalar_tensor_tensor(out=rows[:, t, :], in0=xres[:, t, :], scalar=rstd[:, t:t + 1], in1=fing,
                                               op0=ALU.mult, op1=ALU.mult).then_inc(fin_ready, 1)

        @block.tensor
        def _(pe):
            pe.wait_ge(consts, 1)
            pe.wait_ge(xn_ready, NT)
            for k in range(KD):
                if k >= 2:
                    pe.wait_ge(tr_used_a if k % 2 == 0 else tr_used_v, k // 2)
                for t in range(NT):
                    last = nc.tensor.transpose(pj_bank[k % 2][:, t * P:(t + 1) * P], rows[:, t, k * P:(k + 1) * P],
                                               ident[:])
                last.then_inc(tr_done, 1)
            pe.wait_ge(tr_used_a, KD // 2)
            pe.wait_ge(tr_used_v, KD // 2)
            def transpose_bgu():
                pe.wait_ge(bgu_in, 16)
                for c in range(16):
                    q, r = c // 2, c % 2
                    last = nc.tensor.transpose(pt_bank[0][:, c * NE:(c + 1) * NE],
                                               bgu_rows[:, q * 256 + r:q * 256 + r + 255:2], ident[0:NE, 0:NE])
                last.then_inc(bgu_done, 1)

            def forget_logits():
                pe.wait_ge(f_in, 32)
                for k in range(KD):
                    last = nc.tensor.matmul(pt_bank[1][0:HEADS, :], w_f[:, k, :], colsT[:, k, :],
                                            start=(k == 0), stop=(k == KD - 1))
                last.then_inc(f_done, 1)

            def project(n):
                g, c = n // 4, n % 4
                w = mix_tile(g)
                if c == 0:
                    pe.wait_ge(landed[g % MIX_SLOTS], 16 * (g // MIX_SLOTS + 1))
                if n >= 2:
                    pe.wait_ge(proj_read, n - 1)
                ps = pj_bank[n % 2]
                for k in range(KD):
                    if g in (2, 5):
                        last = nc.tensor.matmul(ps[:, :], colsT[:, k, c * P:(c + 1) * P], w[:, k, :],
                                                start=(k == 0), stop=(k == KD - 1))
                    else:
                        last = nc.tensor.matmul(ps[:, :], w[:, k, c * P:(c + 1) * P], colsT[:, k, :],
                                                start=(k == 0), stop=(k == KD - 1))
                last.then_inc(proj_done, 1)

            def scores(n):
                g, _, t = tile_of(2 * n)
                if n == 0:
                    pe.wait_ge(proj_read, 8)
                    pe.wait_ge(consts, 13)
                if n == 16:
                    pe.wait_ge(proj_read, 20)
                if n >= 1:
                    pe.wait_ge(arg_ready, 2 * n)
                for lo, hi in ((0, t * P), (t * P, (t + 1) * P)):
                    if lo == hi:
                        continue
                    for j in (0, 1):
                        h = tile_of(2 * n + j)[1]
                        c, r = (0 if g == 0 else 8) + h // 2, slice(j * DH, (j + 1) * DH)
                        nc.tensor.matmul(sc_bank[j][:, lo:hi], qk[r, c, t * P:(t + 1) * P], qk[r, c + 4, lo:hi],
                                         start=True, stop=(lo < t * P))
                for j in (0, 1):
                    nc.tensor.matmul(sc_bank[j][:, t * P:(t + 1) * P], identb[:],
                                     (mask_strict if g == 0 else mask_causal)[:], start=False, stop=True
                                     ).then_inc(score_done, 1)

            def transpose_prob(u):
                g, h, t = tile_of(u)
                if g == 0:
                    pe.wait_ge(prob_ready, u + 1)
                else:
                    pe.wait_ge(scaled, u - 31)
                if u >= 2:
                    if u - 2 < 32:
                        pe.wait_ge(probT_v, u - 1)
                    else:
                        pe.wait_ge(probT_a, u - 33)
                for s in range(t + 1):
                    last = nc.tensor.transpose(pt_bank[u % 2][:, s * P:(s + 1) * P],
                                               prob_tile(u)[:, s * P:(s + 1) * P], ident[:])
                last.then_inc(probT_done, 1)

            def attend(n):
                g, _, t = tile_of(2 * n)
                c = n // NT
                if g == 0:
                    pe.wait_ge(probT_v, 2 * n + 2)
                else:
                    pe.wait_ge(probT_a, 2 * n - 30)
                if t == 0 and c >= 2:
                    pe.wait_ge(y_ready, c - 1)
                pe.wait_ge(proj_read, 8 + t + 1 if g == 0 else 20 + t + 1)
                for s in range(t + 1):
                    for j in (0, 1):
                        o = (GW if g == 0 else 0) + tile_of(2 * n + j)[1] * DH
                        last = nc.tensor.matmul(pv_bank[c % 2][j * DH:(j + 1) * DH, t * P:(t + 1) * P],
                                                v_sb[:, s, o:o + DH], wk[:, 6 + j, s * P:(s + 1) * P],
                                                start=(s == 0), stop=(s == t))
                last.then_inc(pv_done, 1)

            def sum_squares(g):
                pe.wait_ge(sq_summed, 4 * (g + 1))
                if g == 1:
                    pe.wait_ge(x1_ready, 8)
                for t in range(NT):
                    last = nc.tensor.matmul(pj_bank[0][:, 2 * t:2 * t + 2], sqsum[:, t * P:(t + 1) * P], onescol[:],
                                            start=True, stop=True)
                last.then_inc(ssy_done, 1)

            def project_out(m):
                g, t, half = m // 8, (m % 8) // 2, m % 2
                if m % 8 == 0:
                    n = 6 + g
                    pe.wait_ge(landed[n % MIX_SLOTS], 16 * (n // MIX_SLOTS + 1))
                    pe.wait_ge(y_ready, 4 * (g + 1))
                    pe.wait_ge(msq_ready, 5 + g)
                if m >= 2:
                    pe.wait_ge(x1_ready, m - 1)
                w = mix_tile(6 + g)
                for k in range(4):
                    last = nc.tensor.matmul(pj_bank[m % 2][:, :], yT[:, (4 if g == 0 else 0) + k, t * P:(t + 1) * P],
                                            w[:, k, half * 512:half * 512 + 512], start=(k == 0), stop=(k == 3))
                last.then_inc(op_done, 1)

            for n in range(8):
                project(n)
            transpose_bgu()
            forget_logits()
            for n in range(NU // 2 + 3):
                if n < 16:
                    project(8 + n)
                if n < NU // 2:
                    scores(n)
                for u in (2 * n - 2, 2 * n - 1):
                    if 0 <= u < NU:
                        if u == 0:
                            pe.wait_ge(bgu_read, 1)
                            pe.wait_ge(zf_ready, 1)
                        transpose_prob(u)
                if 0 <= n - 2 < NU // 2:
                    attend(n - 2)
                if n == 21:
                    sum_squares(0)
                if 23 <= n < 31:
                    project_out(n - 23)
            sum_squares(1)

            def transpose_h2(t):
                pe.wait_ge(x1_ready, 8 + 2 * (t + 1))
                for hf in range(2):
                    if t >= 1:
                        pe.wait_ge(h2t_read, 2 * t - 1 + hf)
                    for k in range(4):
                        kk = 4 * hf + k
                        last = nc.tensor.transpose(pt_bank[hf][:, k * P:(k + 1) * P], xres[:, t, kk * P:(kk + 1) * P],
                                                   ident[:])
                    last.then_inc(h2t_done, 1)

            def router(t):
                pe.wait_ge(h2t_read, 2 * t + 2)
                pe.wait_ge(r_in, 32)
                if t >= 2:
                    pe.wait_ge(rt_read, t - 1)
                for k in range(KD):
                    last = nc.tensor.matmul(sc_bank[t % 2][:, 0:NE], h2T[:, k, t * P:(t + 1) * P], w_r[:, k, :],
                                            start=(k == 0), stop=(k == KD - 1))
                last.then_inc(rt_done, 1)

            for t in range(NT):
                project_out(8 + 2 * t)
                project_out(9 + 2 * t)
                if t > 0:
                    transpose_h2(t - 1)
                if t > 1:
                    router(t - 2)
            transpose_h2(NT - 1)
            router(NT - 2)
            router(NT - 1)

            pe.wait_ge(mask_ready, NT)
            pe.wait_ge(x1_ready, 4 * NT)
            for t in range(NT + 1):
                top = min(t, NT - 1)
                for s in range(top + 1):
                    last = nc.tensor.matmul(pj_bank[0][:, t * NE:(t + 1) * NE], (before if s == t else ones)[:],
                                            maskb[:, s, :], start=(s == 0), stop=(s == top))
            last.then_inc(rank_done, 1)
            def transpose_gates():
                pe.wait_ge(gate_ready, NT)
                pe.wait_ge(h2t_read, 2 * NT)
                gv = gate_et[:].rearrange("p (e t) -> p t e", t=NT)
                for t in range(NT):
                    last = nc.tensor.transpose(pt_bank[0][0:NE, t * P:(t + 1) * P], gv[:, t, :], ident[:])
                last.then_inc(gt_done, 1)

            def slot_rows():
                for t in range(NT):
                    last = nc.tensor.matmul(pj_bank[0][0:BLK, 0:4], sel[:, t, :], info[:, t, :],
                                            start=(t == 0), stop=(t == NT - 1))
                last.then_inc(idx_done, 1)

            def transpose_x():
                for k in range(KD):
                    hf, kk = k // 4, k % 4
                    last = nc.tensor.transpose(pt_bank[hf][:, kk * BLK:(kk + 1) * BLK], xg[:, k * P:(k + 1) * P],
                                               ident[0:BLK, 0:BLK])
                last.then_inc(xt_done, 1)

            pe.wait_ge(sel_ready, 1)
            slot_rows()
            transpose_gates()
            pe.wait_ge(gt_read, 1)
            pe.wait_ge(bdown_in, 16)
            for m in range(2 * NT):
                t, half = m // 2, m % 2
                if m >= 2:
                    pe.wait_ge(bd_copied, m - 1)
                nc.tensor.matmul(sc_bank[m % 2][:, :], gT[:, t * P:(t + 1) * P], bdown_sb[:, half * 512:half * 512 + 512],
                                 start=True, stop=True).then_inc(bd_done, 1)
            pe.wait_ge(gathered, 16)
            transpose_x()
            pe.wait_ge(bd_copied, 2 * NT)
            pe.wait_ge(items_ready, 1)

            n_items = pe.value_load(n_items_sb[0:1, 0:1], min_val=NE, max_val=NE + EXTRA_MAX)
            with pe.Fori(0, n_items) as i:
                pe.wait_ge(xt_ready, i + 1)
                for q in range(4):
                    pe.wait_ge(landed[q], i * 16 + 48)
                    pe.wait_ge(gu_used, i * 4 + (q + 1))
                    w = gu_tile(q)
                    for jj in range(2):
                        for r in range(2):
                            o = (2 * jj + r) * BLK
                            for k in range(KD):
                                last = nc.tensor.matmul(sc_bank[q % 2][:, o:o + BLK],
                                                        w[:, k, jj * 256 + r:jj * 256 + r + 255:2], xgT[:, k, :],
                                                        start=(k == 0), stop=(k == KD - 1))
                    last.then_inc(gu_done, 1)
                    if q == 0:
                        pe.wait_ge(sel_ready, i + 2)
                        slot_rows()
                few = pe.value_load(item_few[0:1, bass.ds(i, 1)], min_val=0, max_val=1)

                def down(rows, first):
                    for k in range(KD):
                        if k % 4 == 0:
                            pe.wait_ge(landed[4 + k // 4], i * 16 + 16)
                        if k % 2 == 0:
                            pe.wait_ge(act_ready, i * 4 + (k // 2 + 1))
                        if k == 0:
                            pe.wait_ge(y0_ready, i + NT)
                            pe.wait_ge(y1_ready, i + 1)
                        if k == 4:
                            pe.wait_ge(gathered, i * 16 + 32)
                            transpose_x()
                        w = down_tile(k // 4)
                        for half in range(2):
                            last = nc.tensor.matmul(pv_bank[half][first[half]:first[half] + rows, :], actT[:, k, 0:rows],
                                                    w[:, k % 4, half * 512:half * 512 + 512],
                                                    start=(k == 0), stop=(k == KD - 1))
                        if k == 3:
                            last.then_inc(half_done, 1)
                    last.then_inc(down_done, 1)

                with pe.If(few):
                    down(FEW, (0, P // 2))
                with pe.Else():
                    down(BLK, (0, 0))


_INS = ["x", "attn_norm_g", "w_in", "b_forget", "fox_out_g", "sb_out_g", "w_out", "ffn_norm_g", "w_router", "b_router",
        "w_gate_up", "b_gate_up", "w_down", "b_down", "final_norm_g"]


def kernel(**inputs):
    import numpy as _np
    import concourse.bacc as _bacc
    from concourse import mybir as _mybir
    from concourse.bass_utils import run_bass_kernel_spmd as _run

    nc = _bacc.Bacc("TRN2", target_bir_lowering=False, num_devices=1)
    arrays, args = {}, []
    for name in _INS:
        a = _np.ascontiguousarray(inputs[name])
        arrays[f"in_{name}_dram"] = a
        args.append(nc.dram_tensor(f"in_{name}_dram", a.shape, _mybir.dt.from_np(a.dtype), kind="ExternalInput").ap())
    args.append(nc.dram_tensor("out_0_dram", (1, SEQ, D), _mybir.dt.float32, kind="ExternalOutput").ap())
    hybrid_layer(nc, *args)
    r = _run(nc, [arrays], core_ids=[0])
    return r.results[0]["out_0_dram"]
```

```python
from contextlib import ExitStack

import concourse.bass as bass
from concourse import mybir

P = 128
D = 1024
SEQ = 512
NT = SEQ // P
KD = D // P
HEADS = 8
DH = 64
GW = HEADS * DH
NE = 32
TOPK = 4
FF = 1024
BLK = 104
FEW = 64
LIMIT = 7.0
ALPHA = 1.702
EPS = 1e-5
SCALE = 1.0 / DH ** 0.5

PIECE = 4096
SLOTS = 6
MIX_SLOTS = 4
MIX_PIECES = 8
TWICE = 3
EXTRA_MAX = SEQ * TOPK // BLK
MAXBLK = -(-SEQ // BLK)
NX = EXTRA_MAX + 2 + (NE + EXTRA_MAX) % 2
NI = NE + NX
FAR = 4096.0
NEG = -1e30

ALU = mybir.AluOpType
ACT = mybir.ActivationFunctionType
AX = mybir.AxisListType
F32 = mybir.dt.float32
BF16 = mybir.dt.bfloat16
I32 = mybir.dt.int32
U32 = mybir.dt.uint32


def hybrid_layer(nc, x, attn_norm_g, w_in, b_forget, fox_out_g, sb_out_g, w_out, ffn_norm_g,
                 w_router, b_router, w_gate_up, b_gate_up, w_down, b_down, final_norm_g, out):
    ctx = ExitStack()
    with ctx:
        def sb(name, shape, dt=F32):
            return ctx.enter_context(nc.sbuf_tensor(name, shape, dt))

        def sem(name):
            return ctx.enter_context(nc.semaphore(name))

        h2_rows = nc.dram_tensor("h2_rows", [SEQ + P, D], F32, kind="Internal").ap()
        acc_rows = nc.dram_tensor("acc_rows", [SEQ + P, D], F32, kind="Internal").ap()
        negc_rows = nc.dram_tensor("negc_rows", [HEADS, SEQ], F32, kind="Internal").ap()

        ring = sb("ring", [P, SLOTS, PIECE])
        xres = sb("xres", [P, NT, D])
        rows_buf = sb("rows_buf", [P, NT * D])
        cols_buf = sb("cols_buf", [P, NT * D])
        big = sb("big", [P, 12288])

        def part(base, *dims):
            n = 1
            for d in dims:
                n *= d
            v = base
            if len(dims) == 2:
                return v.rearrange("p (a b) -> p a b", b=dims[1])
            if len(dims) == 3:
                return v.rearrange("p (a b c) -> p a b c", b=dims[1], c=dims[2])
            return v

        rows = part(rows_buf[:], NT, D)
        yT = part(rows_buf[:], KD, SEQ)
        colsT = part(cols_buf[:], KD, SEQ)
        h2 = part(cols_buf[:], NT, D)
        qk = part(big[:, 0:8192], 16, SEQ)
        v_sb = part(big[:, 8192:12288], NT, 2 * GW)
        forget_rows = part(big[0:HEADS, 4096:4096 + 4 * SEQ], 4, SEQ)
        bgu_rows = big[0:NE, 8192:8192 + 2 * FF]
        negc = part(ring[:, 4, :], HEADS, SEQ)
        wk = part(ring[:, 5, :], 8, SEQ)
        zrow = ring[:, 5, 0:D]

        h2T = part(big[:, 0:4096], KD, SEQ)
        onehot = part(big[:, 4096:4608], NT, TOPK, NE)
        onehot_g = part(big[:, 4608:5120], NT, TOPK, NE)
        ident3 = big[0:3 * NE, 5248:5280]
        esel = big[0:3 * NE, 5120:5120 + BLK // 2].bitcast(BF16)
        bdown_sb = big[0:3 * NE, 5632:6656]
        itemcmp = part(big[:, 6656:6656 + NX * NE], NX, NE)
        itemcmp2 = part(big[:, 7424:7424 + NX * NE], NX, NE)
        gu_rows = part(big[:, 2304:3328], 2, 512)
        xg = big[0:BLK, 8192:9216]
        xgT = part(big[:, 9216:9216 + KD * BLK], KD, BLK)
        actT = part(big[:, 10240:10240 + KD * BLK], KD, BLK)
        ysb = big[0:BLK, 11264:12288]
        gtile = [part(big[:, 256 * j:256 * j + 2 * BLK], 2, BLK) for j in range(2)]
        utile = [part(big[:, 512 + 256 * j:512 + 256 * j + 2 * BLK], 2, BLK) for j in range(2)]
        stile = [part(big[:, 1024 + 256 * j:1024 + 256 * j + 2 * BLK], 2, BLK) for j in range(2)]
        fing = big[:, 4096:4096 + D]
        logits = part(big[:, 11264:11392], NT, NE)
        maskf = part(big[:, 11392:11520], NT, NE)
        w_r = part(big[:, 11520:11776], KD, NE)
        sel = part(big[:, 2048:2048 + NT * BLK // 2].bitcast(BF16), NT, BLK)

        ident = sb("ident", [P, P])
        identb = sb("identb", [P, P], BF16)
        mask_causal = sb("mask_causal", [P, P], BF16)
        mask_strict = sb("mask_strict", [P, P], BF16)
        before = sb("before", [P, P], BF16)
        ones = sb("ones", [P, P], BF16)
        g_attn = sb("g_attn", [P, KD])
        g_mix = sb("g_mix", [P, KD])
        g_ffn = sb("g_ffn", [P, KD])
        w_f = sb("w_f", [P, KD, HEADS])
        bf_c = sb("bf_c", [HEADS, 1])
        br_b = sb("br_b", [P, NE])
        bgu = sb("bgu", [P, NE, 16])
        ssq = sb("ssq", [P, 16])
        rstd = sb("rstd", [P, 16])
        msq = sb("msq", [P, 16])
        sq = sb("sq", [P, 2, SEQ])
        gate_rest = sq[:, 1, 0:NE * NT]
        item_half = sq[0:1, 1, 320:320 + NI].bitcast(I32)
        item_odd = sq[0:1, 1, 384:384 + NI].bitcast(I32)
        gate3 = part(sq[:, 1, 128:128 + NE * NT * 3 // 2].bitcast(BF16), NE * NT, 3)
        bdown3 = sq[0:3 * NE, 0, :].bitcast(BF16)
        sqsum = sb("sqsum", [P, SEQ])
        zf = forget_rows[:, 0, :]
        lf = forget_rows[:, 1, :]
        negc_sb = forget_rows[:, 2, :]
        nmax = sb("nmax", [P, 32])
        rsum = sb("rsum", [P, 32])
        rinv = sb("rinv", [P, 32])
        top8 = sb("top8", [P, NT, 8])
        topi = sb("topi", [P, NT, 8], U32)
        topk_places = sb("topk_places", [P, NT * TOPK])
        gexp = sb("gexp", [P, NT, TOPK])
        gsum = sb("gsum", [P, NT])
        ginv = sb("ginv", [P, NT])
        maskb = sb("maskb", [P, NT, NE], BF16)
        gate_et = sb("gate_et", [P, NE * NT])
        rank_et = sb("rank_et", [P, NE * NT])
        counts = sb("counts", [P, NE])
        extra = sb("extra", [P, NE])
        onesrow = sb("onesrow", [P, NE])
        onescol = sb("onescol", [P, 2])
        cumx = sb("cumx", [P, NE])
        iota = sb("iota", [P, P])
        padrow = sb("padrow", [P, 1])
        item_e = sb("item_e", [1, NI], I32)
        item_f = sb("item_f", [P, NI])
        few_before = sb("few_before", [1, NI], I32)
        few_sum = sb("few_sum", [1, NE])
        item_few = sb("item_few", [1, NI], I32)
        item_b = sb("item_b", [P, NI])
        n_items_sb = sb("n_items_sb", [1, 2], I32)
        cxj = sb("cxj", [P, NX])
        rel = sb("rel", [P, NT])
        info = sb("info", [P, NT, 6], BF16)
        idsum = sb("idsum", [BLK, 1])
        biasc = sb("biasc", [P, 16])
        pausing = sb("pausing", [1, 2])
        padsel = sb("padsel", [BLK, 1])
        idx_next = sb("idx_next", [BLK, 1], I32)
        idx_mid = sb("idx_mid", [BLK, 1], I32)
        idx_now = sb("idx_now", [BLK, 1], I32)
        gate_next = sb("gate_next", [BLK, 1])
        gate_mid = sb("gate_mid", [BLK, 1])
        gate_now = sb("gate_now", [BLK, 1])

        bank = [ctx.enter_context(nc.psum_tensor(f"bank{i}", [P, 512], F32)) for i in range(8)]
        sc_bank, pt_bank, pv_bank, pj_bank = bank[0:2], bank[2:4], bank[4:6], bank[6:8]
        logit_bank = sc_bank + pv_bank
        ssq_bank = [pj_bank[0], sc_bank[0]]

        landed = [sem(f"landed{s}") for s in range(SLOTS)]
        landed_odd = [sem(f"landed_odd{j}") for j in range(TWICE)]
        half_ready = sem("half_ready")
        x_in = [sem(f"x_in{t}") for t in range(NT)]
        g_in = sem("g_in")
        f_in = sem("f_in")
        bgu_in = sem("bgu_in")
        r_in = sem("r_in")
        bdown_in = sem("bdown_in")
        bdown_ready = sem("bdown_ready")
        fing_in = sem("fing_in")
        pads_out = sem("pads_out")
        negc_out = sem("negc_out")
        negc_in = sem("negc_in")
        h2_out = sem("h2_out")
        acc_out = sem("acc_out")
        consts = sem("consts")
        zero_ok = sem("zero_ok")
        dstep = sem("dstep")
        astep = sem("astep")
        pstep = sem("pstep")
        xn_ready = sem("xn_ready")
        ssx = sem("ssx")
        tr_done = sem("tr_done")
        tr_used_a = sem("tr_used_a")
        tr_used_v = sem("tr_used_v")
        bgu_done = sem("bgu_done")
        bgu_read = sem("bgu_read")
        f_done = sem("f_done")
        zf_ready = sem("zf_ready")
        lf_abs = sem("lf_abs")
        negc_ready = sem("negc_ready")
        proj_done = sem("proj_done")
        proj_read = sem("proj_read")
        score_done = sem("score_done")
        softln = sem("softln")
        arg_ready = sem("arg_ready")
        prob_ready = sem("prob_ready")
        probT_done = sem("probT_done")
        probT_v = sem("probT_v")
        probT_a = sem("probT_a")
        pv_done = sem("pv_done")
        y_ready = sem("y_ready")
        scaled = sem("scaled")
        sq_ready = sem("sq_ready")
        sq_summed = sem("sq_summed")
        ssy_done = sem("ssy_done")
        op_done = sem("op_done")
        x1_ready = sem("x1_ready")
        ss1 = sem("ss1")
        h2_ready = sem("h2_ready")
        h2t_done = sem("h2t_done")
        h2t_read = sem("h2t_read")
        rt_done = sem("rt_done")
        gl_ready = sem("gl_ready")
        mask_ready = sem("mask_ready")
        rank_done = sem("rank_done")
        count_ready = sem("count_ready")
        items_ready = sem("items_ready")
        sel_ready = sem("sel_ready")
        idx_done = sem("idx_done")
        idx_ready = sem("idx_ready")
        gathered = sem("gathered")
        xt_done = sem("xt_done")
        xt_ready = sem("xt_ready")
        gu_done = sem("gu_done")
        gu_used = sem("gu_used")
        g_ready = sem("g_ready")
        s_ready = sem("s_ready")
        act_ready = sem("act_ready")
        half_done = sem("half_done")
        down_done = sem("down_done")
        rows_done = sem("rows_done")
        esel_ready = sem("esel_ready")
        rows_read = sem("rows_read")
        bias_ready = sem("bias_ready")
        rel_ready = sem("rel_ready")
        u_step = sem("u_step")
        now_ready = sem("now_ready")
        pad_step = sem("pad_step")
        paused = sem("paused")
        rt_read = sem("rt_read")
        msq_ready = sem("msq_ready")
        root_ready = sem("root_ready")
        y0_ready = sem("y0_ready")
        y1_ready = sem("y1_ready")
        scattered = sem("scattered")
        ssf = sem("ssf")
        fin_ready = sem("fin_ready")
        stored = sem("stored")

        OFF_F = 3 * GW
        OFF_B = OFF_F + HEADS
        mix_cols = [OFF_B, OFF_B + GW, OFF_B + 2 * GW, 0, GW, 2 * GW]

        def mix_source(n):
            if n < 6:
                return w_in[:, mix_cols[n]:mix_cols[n] + GW].rearrange("(k p) c -> p k c", p=P)
            r = GW if n == 6 else 0
            return w_out[r:r + GW, :].rearrange("(k p) c -> p k c", p=P)

        def mix_tile(n):
            return part(ring[:, n % MIX_SLOTS, :], *((KD, 512) if n < 6 else (4, D)))

        odd_buf = [rows_buf[:], cols_buf[:], xres[:].rearrange("p t d -> p (t d)")]

        def gu_tile(q, odd):
            return part(odd_buf[q] if odd and q < TWICE else ring[:, q, :], KD, 512)

        def down_tile(h):
            return part(ring[:, 4 + h, :], 4, D)

        NU = 2 * HEADS * NT
        NPAIR = HEADS
        OUT_B_STEPS = [20, 21, 22, 24, 26, 28, 30, 33]

        def tile_of(u):
            r = u % 32
            return u // 32, 2 * (r // 8) + r % 2, (r % 8) // 2

        def prob_tile(u):
            return wk[:, 4 + u % 2, :] if u < 32 else wk[:, u % 4, :]

        block = ctx.enter_context(nc.Block())

        @block.sync
        def _(sp):
            xv = x[0].rearrange("(t p) d -> p t d", p=P)
            for t in range(NT):
                sp.dma_start(xres[:, t, :], xv[:, t, :]).then_inc(x_in[t], 16)
            for n in range(MIX_PIECES):
                if n >= MIX_SLOTS:
                    sp.wait_ge(proj_done, 4 * (n - MIX_SLOTS + 1))
                sp.dma_start(mix_tile(n), mix_source(n)).then_inc(landed[n % MIX_SLOTS], 16)

            def load_piece(e, j, odd):
                which = slice(e, e + 1) if isinstance(e, int) else bass.ds(e, 1)
                if j < 4:
                    src = w_gate_up[which, :, j * 512:(j + 1) * 512]
                    dst = gu_tile(j, odd)
                else:
                    src = w_down[which, (j - 4) * 512:(j - 3) * 512, :]
                    dst = down_tile(j - 4)
                sp.dma_start(dst, src.rearrange("a (k p) c -> p (a k) c", p=P)
                             ).then_inc((landed_odd if odd and j < TWICE else landed)[j], 16)

            for j in (0, 1):
                sp.wait_ge(proj_done, 4 * (4 + j + 1))
                load_piece(0, j, False)
            sp.wait_ge(y_ready, NPAIR)
            for j in (4, 5):
                load_piece(0, j, False)
            for j in (2, 3):
                sp.wait_ge(op_done, 2 * NT * (j - 1))
                load_piece(0, j, False)
            sp.wait_ge(op_done, 4 * NT)
            load_piece(1, 0, True)
            sp.wait_ge(gathered, 16)
            sp.wait_ge(h2_out, 16 * NT)
            load_piece(1, 1, True)
            sp.wait_ge(acc_out, 16 * NT)
            sp.wait_ge(h2t_done, 2 * NT)
            sp.wait_ge(h2_ready, NT)
            load_piece(1, 2, True)
            sp.wait_ge(items_ready, 1)
            sp.wait_ge(half_ready, 1)
            n_items = sp.value_load(n_items_sb[0:1, 0:1], min_val=NE, max_val=NE + EXTRA_MAX)

            def last_pieces(e, i):
                sp.wait_ge(gu_done, i * 4)
                load_piece(e, 3, False)
                sp.wait_ge(half_done, i)
                load_piece(e, 4, False)
                sp.wait_ge(down_done, i)
                load_piece(e, 5, False)

            with sp.Fori(2, n_items) as i:
                e = sp.value_load(item_e[0:1, bass.ds(i, 1)], min_val=0, max_val=NE - 1)
                e_before = sp.value_load(item_e[0:1, bass.ds(i - 1, 1)], min_val=0, max_val=NE - 1)
                odd = sp.value_load(item_odd[0:1, bass.ds(i, 1)], min_val=0, max_val=1)

                def first_pieces(is_odd):
                    for j in range(TWICE):
                        sp.wait_ge(gu_done, i * 4 + (j - 7))
                        load_piece(e, j, is_odd)

                with sp.If(odd):
                    first_pieces(True)
                with sp.Else():
                    first_pieces(False)
                last_pieces(e_before, i - 1)
            i_last = sp.value_load(n_items_sb[0:1, 1:2], min_val=NE - 1, max_val=NE + EXTRA_MAX - 1)
            e_last = sp.value_load(item_e[0:1, bass.ds(i_last, 1)], min_val=0, max_val=NE - 1)
            last_pieces(e_last, i_last)

            ov = out[0].rearrange("(t p) d -> p t d", p=P)
            for t in range(NT):
                sp.wait_ge(fin_ready, t + 1)
                sp.dma_start(ov[:, t, :], rows[:, t, :]).then_inc(stored, 16)
            sp.wait_ge(stored, 16 * NT)

        @block.gpsimd
        def _(pool):
            chain = [0]

            def link(ins):
                chain[0] += 1
                ins.then_inc(pstep, 1)
                pool.wait_ge(pstep, chain[0])

            def tri(dst, keep, fill, op, step, mult, width=P):
                link(nc.gpsimd.memset(dst, keep))
                return nc.gpsimd.affine_select(out=dst, in_=dst, compare_op=op, fill=fill, base=0,
                                               pattern=[[step, width]], channel_multiplier=mult)

            tri(ident[:], 0.0, 1.0, ALU.not_equal, -1, 1).then_inc(consts, 1)
            nc.gpsimd.memset(zrow, 0.0).then_inc(zero_ok, 1)
            nc.gpsimd.memset(onescol[:], 1.0).then_inc(consts, 1)
            tri(identb[:], 0.0, 1.0, ALU.not_equal, -1, 1).then_inc(consts, 1)
            tri(mask_strict[:], 0.0, NEG, ALU.is_gt, -1, 1).then_inc(consts, 1)
            tri(mask_causal[:], 0.0, NEG, ALU.is_ge, -1, 1).then_inc(consts, 1)
            tri(before[:], 1.0, 0.0, ALU.is_gt, 1, -1).then_inc(consts, 1)
            nc.gpsimd.memset(ones[:], 1.0).then_inc(consts, 1)
            nc.gpsimd.memset(onesrow[:], 1.0).then_inc(consts, 1)
            link(nc.gpsimd.memset(info[:], 1.0))
            nc.gpsimd.iota(iota[:], [[1, P]], base=0, channel_multiplier=0,
                           allow_small_or_imprecise_dtypes=True).then_inc(consts, 1)
            nc.gpsimd.iota(padrow[:], [[1, 1]], base=SEQ, channel_multiplier=1,
                           allow_small_or_imprecise_dtypes=True).then_inc(consts, 1)
            for t in range(NT):
                ins = nc.gpsimd.memset(info[:, t, 0:1], float(t * P))
            link(ins)
            nc.gpsimd.iota(info[:, :, 1], [[0, NT]], base=0, channel_multiplier=1,
                           allow_small_or_imprecise_dtypes=True).then_inc(consts, 1)
            nc.gpsimd.iota(item_f[:], [[1, NI]], base=0, channel_multiplier=0,
                           allow_small_or_imprecise_dtypes=True).then_inc(consts, 1)
            nc.gpsimd.memset(item_few[:], 0)
            nc.gpsimd.memset(few_before[:], 0)
            nc.gpsimd.memset(item_b[:], -FAR).then_inc(consts, 1)
            nc.gpsimd.memset(pausing[:], 0.0).then_inc(paused, 1)
            pool.wait_ge(zero_ok, 1)
            pool.dma_start(acc_rows[SEQ:SEQ + P, :], zrow).then_inc(scattered, 16)

            for c in range(NPAIR):
                pool.wait_ge(sq_ready, c + 1)
                if c == 4:
                    pool.wait_ge(ssy_done, 1)
                if c % 4 == 0:
                    ins = nc.gpsimd.tensor_copy(sqsum[:], sq[:, c % 2, :])
                else:
                    ins = nc.gpsimd.tensor_tensor(sqsum[:], sqsum[:], sq[:, c % 2, :], ALU.add)
                ins.then_inc(sq_summed, 1)
                pool.wait_ge(sq_summed, c + 1)

            def pause(c):
                nc.gpsimd.tensor_tensor(pausing[:, c:c + 1], onesrow[0:1, 0:1], onesrow[0:1, 0:1], ALU.add
                                        ).then_inc(paused, 1)

            def gather(idx, rows):
                pool.indirect_dma_start(out=xg[0:rows], out_offset=None, in_=h2_rows,
                                        in_offset=bass.IndirectOffsetOnAxis(ap=idx[0:rows, 0:1], axis=0)
                                        ).then_inc(gathered, 16)

            def scatter(rows):
                pool.indirect_dma_start(out=acc_rows, out_offset=bass.IndirectOffsetOnAxis(ap=idx_now[0:rows, 0:1], axis=0),
                                        in_=ysb[0:rows], in_offset=None, compute_op=ALU.add).then_inc(scattered, 16)

            pool.wait_ge(bdown_in, 48)
            link(nc.gpsimd.tensor_tensor(ident3, ident[0:3 * NE, 0:NE], ident[0:3 * NE, NE:2 * NE], ALU.add))
            link(nc.gpsimd.tensor_tensor(ident3, ident3, ident[0:3 * NE, 2 * NE:3 * NE], ALU.add))
            link(nc.gpsimd.tensor_copy(bdown3, bdown_sb))
            for p0, p1 in ((NE, 2 * NE), (2 * NE, 3 * NE), (2 * NE, 3 * NE)):
                link(nc.gpsimd.tensor_tensor(bdown_sb[p0:p1], bdown_sb[p0:p1], bdown3[p0:p1], ALU.subtract))
                link(nc.gpsimd.tensor_copy(bdown3[p0:p1], bdown_sb[p0:p1]))
            nc.gpsimd.iota(item_half, [[1, NI // 2], [0, 2]], base=0, channel_multiplier=0)
            nc.gpsimd.iota(item_odd, [[0, NI // 2], [1, 2]], base=0, channel_multiplier=0).then_inc(half_ready, 1)
            nc.gpsimd.memset(pausing[:], 0.0).then_inc(bdown_ready, 1)
            pool.wait_ge(bdown_ready, 1)

            pool.wait_ge(h2_out, 16 * NT)
            pool.wait_ge(pads_out, 16)
            pool.wait_ge(idx_ready, 1)
            gather(idx_mid, BLK)
            pool.wait_ge(xt_done, 1)
            pool.wait_ge(idx_ready, 2)
            gather(idx_next, BLK)
            pool.wait_ge(acc_out, 16 * NT)
            pool.wait_ge(count_ready, 1)
            n_items = pool.value_load(n_items_sb[0:1, 0:1], min_val=NE, max_val=NE + EXTRA_MAX)
            with pool.Fori(0, n_items) as i:
                pool.wait_ge(paused, i * 2 + 1)
                pool.wait_ge(idx_ready, i + 3)
                pool.wait_ge(xt_done, i + 2)
                pause(0)
                few_later = pool.value_load(item_few[0:1, bass.ds(i + 2, 1)], min_val=0, max_val=1)
                with pool.If(few_later):
                    gather(idx_next, FEW)
                with pool.Else():
                    gather(idx_next, BLK)
                pool.wait_ge(y0_ready, i + (NT + 1))
                pool.wait_ge(y1_ready, i + 2)
                pool.wait_ge(scattered, i * 16 + 16)
                pause(1)
                few = pool.value_load(item_few[0:1, bass.ds(i, 1)], min_val=0, max_val=1)
                with pool.If(few):
                    scatter(FEW)
                with pool.Else():
                    scatter(BLK)
            pool.wait_ge(scattered, n_items * 16 + 16)
            pool.wait_ge(gathered, n_items * 16 + 32)

        @block.scalar
        def _(act):
            chain = [0]

            def link(ins):
                chain[0] += 1
                ins.then_inc(astep, 1)
                act.wait_ge(astep, chain[0])

            root_count = [0]

            def root(col, n):
                c = slice(col, col + n)
                root_count[0] += 1
                act.wait_ge(msq_ready, root_count[0])
                link(nc.scalar.activation(msq[:, c], msq[:, c], ACT.Ln))
                nc.scalar.activation(rstd[:, c], msq[:, c], ACT.Exp, scale=0.5).then_inc(root_ready, 1)

            nc.scalar.preload_act_table_set("natural_log_exp_and_others")
            with nc.allow_non_contiguous_dma(reason="gains, one per partition"):
                act.dma_start(g_attn[:], attn_norm_g.rearrange("(k p) -> p k", p=P)).then_inc(g_in, 16)
                act.dma_start(g_mix[:, 0:4], fox_out_g.rearrange("(k p) -> p k", p=P)).then_inc(g_in, 16)
                act.dma_start(g_mix[:, 4:8], sb_out_g.rearrange("(k p) -> p k", p=P)).then_inc(g_in, 16)
                act.dma_start(g_ffn[:], ffn_norm_g.rearrange("(k p) -> p k", p=P)).then_inc(g_in, 16)
                act.dma_start(w_f[:], w_in[:, OFF_F:OFF_F + HEADS].rearrange("(k p) c -> p k c", p=P)).then_inc(f_in, 16)
                act.dma_start(bf_c[:], b_forget.rearrange("(h a) -> h a", a=1)).then_inc(f_in, 16)
            act.dma_start(bgu_rows, b_gate_up).then_inc(bgu_in, 16)
            act.dma_start(br_b[:], b_router.rearrange("(a h) -> a h", a=1).to_broadcast([P, NE])).then_inc(r_in, 16)
            act.wait_ge(zero_ok, 1)
            act.dma_start(h2_rows[SEQ:SEQ + P, :], zrow).then_inc(pads_out, 16)

            for t in range(NT):
                act.wait_ge(x_in[t], 16)
                nc.scalar.activation(rows[:, t, :], xres[:, t, :], ACT.Square, accum_out=ssq[:, t:t + 1]).then_inc(ssx, 1)
                root(t, 1)

            act.wait_ge(g_in, 64)
            for k in range(0, KD, 2):
                act.wait_ge(tr_done, k + 1)
                nc.scalar.activation(colsT[:, k, :], pj_bank[0][:, :], ACT.Copy, scale=g_attn[:, k:k + 1]
                                     ).then_inc(tr_used_a, 1)

            def forget():
                act.wait_ge(zf_ready, 1)
                link(nc.scalar.activation(lf, zf, ACT.Abs))
                link(nc.scalar.activation(lf, lf, ACT.Exp, scale=-1.0))
                nc.scalar.activation(lf, lf, ACT.Ln, bias=1.0).then_inc(lf_abs, 1)

            def negc_copy():
                act.wait_ge(negc_ready, 1)
                act.dma_start(negc_rows, negc_sb).then_inc(negc_out, 16)
                act.wait_ge(negc_out, 16)
                src = negc_rows.rearrange("(a h) s -> a (h s)", a=1).to_broadcast([P, HEADS * SEQ])
                act.dma_start(ring[:, 4, :], src).then_inc(negc_in, 16)

            def read_proj(n):
                act.wait_ge(proj_done, n + 1)
                ps = pj_bank[n % 2]
                g, c = n // 4, n % 4
                if g in (2, 5):
                    dst = v_sb[:, c, (GW if g == 2 else 0):(GW if g == 2 else 0) + GW]
                    ins = nc.scalar.copy(dst, ps[:, :])
                else:
                    slot = {0: 0, 1: 4, 3: 8, 4: 12}[g] + c
                    if g in (0, 3):
                        ins = nc.scalar.activation(qk[:, slot, :], ps[:, :], ACT.Copy, scale=SCALE)
                    else:
                        ins = nc.scalar.copy(qk[:, slot, :], ps[:, :])
                ins.then_inc(proj_read, 1)

            def soft(u):
                g, h, t = tile_of(u)
                w = (t + 1) * P
                act.wait_ge(score_done, u + 1)
                if u == 0:
                    act.wait_ge(pads_out, 16)
                    act.wait_ge(scattered, 16)
                if u >= 2:
                    act.wait_ge(arg_ready, u - 1)
                link(nc.scalar.activation(wk[:, u % 2, 0:w], sc_bank[u % 2][:, 0:w], ACT.Abs))
                link(nc.scalar.activation(wk[:, u % 2, 0:w], wk[:, u % 2, 0:w], ACT.Exp, scale=-1.0))
                nc.scalar.activation(wk[:, u % 2, 0:w], wk[:, u % 2, 0:w], ACT.Ln, bias=1.0).then_inc(softln, 1)

            def prob(u):
                g, h, t = tile_of(u)
                w = (t + 1) * P
                act.wait_ge(arg_ready, u + 1)
                p = prob_tile(u)[:, 0:w]
                if g == 0:
                    nc.scalar.activation(p, p, ACT.Exp).then_inc(prob_ready, 1)
                else:
                    c = u - 32
                    nc.scalar.activation(p, p, ACT.Exp, scale=-1.0,
                                         bias=nmax[:, c:c + 1], accum_out=rsum[:, c:c + 1]).then_inc(prob_ready, 1)

            def copy_probT(u):
                g, h, t = tile_of(u)
                w = (t + 1) * P
                act.wait_ge(probT_done, u + 1)
                act.wait_ge(pv_done, u // 2)
                nc.scalar.copy(wk[:, 6 + u % 2, 0:w], pt_bank[u % 2][:, 0:w]).then_inc(probT_a, 1)

            def square(c):
                act.wait_ge(pv_done, 4 * (c + 1))
                if c >= 2:
                    act.wait_ge(sq_summed, c - 1)
                nc.scalar.activation(sq[:, c % 2, :], pv_bank[c % 2][:, :], ACT.Square).then_inc(sq_ready, 1)

            for n in range(8):
                read_proj(n)
            forget()
            for n in range(NU // 2 + 3):
                if 1 <= n <= 16:
                    prob(2 * n - 1)
                if n < 16:
                    read_proj(8 + n)
                    soft(2 * n)
                    soft(2 * n + 1)
                    prob(2 * n)
                if n == 1:
                    negc_copy()
                for j in (0, 1):
                    if 16 <= n < NU // 2:
                        prob(2 * n + j)
                for j in (0, 1):
                    if 32 <= 2 * n - 2 + j < NU:
                        copy_probT(2 * n - 2 + j)
                if n >= 6 and (n - 6) % 4 == 0:
                    square((n - 6) // 4)
                if n == 20:
                    root(4, 4)
            root(8, 4)

            act.wait_ge(y_ready, NPAIR)
            act.dma_start(w_r, w_router.rearrange("(k p) c -> p k c", p=P)).then_inc(r_in, 16)
            for c in range(3):
                act.dma_start(bdown_sb[c * NE:(c + 1) * NE], b_down).then_inc(bdown_in, 16)

            for t in range(NT):
                act.wait_ge(x1_ready, 2 * NT + 2 * (t + 1))
                nc.scalar.activation(h2[:, t, :], xres[:, t, :], ACT.Square,
                                     accum_out=ssq[:, 12 + t:13 + t]).then_inc(ss1, 1)
                root(12 + t, 1)
                act.wait_ge(h2_ready, t + 1)
                act.dma_start(h2_rows[t * P:(t + 1) * P, :], h2[:, t, :]).then_inc(h2_out, 16)

            def gate_exp(t):
                act.wait_ge(gl_ready, t + 1)
                nc.scalar.activation(gexp[:, t, :], gexp[:, t, :], ACT.Exp).then_inc(y0_ready, 1)

            for t in range(NT):
                gate_exp(t)
            act.wait_ge(gathered, 16)
            for t in range(NT):
                act.dma_start(acc_rows[t * P:(t + 1) * P, :], xres[:, t, :]).then_inc(acc_out, 16)

            act.wait_ge(count_ready, 1)
            n_items = act.value_load(n_items_sb[0:1, 0:1], min_val=NE, max_val=NE + EXTRA_MAX)
            with act.Fori(0, n_items) as i:
                few = act.value_load(item_few[0:1, bass.ds(i, 1)], min_val=0, max_val=1)
                before_i = act.value_load(few_before[0:1, bass.ds(i, 1)], min_val=0, max_val=NE)

                def sigmoid(q):
                    act.wait_ge(g_ready, i * 4 + (q + 1))
                    nc.scalar.activation(stile[q % 2], gtile[q % 2], ACT.Sigmoid, scale=ALPHA).then_inc(s_ready, 1)

                with act.If(few):
                    for p in range(2):
                        act.wait_ge(rows_done, before_i * 2 + (p + 1))
                        nc.scalar.copy(gu_rows[:, p, :], pt_bank[p][:, :]).then_inc(rows_read, 1)
                        sigmoid(2 * p)
                        sigmoid(2 * p + 1)
                with act.Else():
                    for q in range(4):
                        sigmoid(q)
                act.wait_ge(down_done, i + 1)
                act.wait_ge(idx_ready, i + 3)
                act.wait_ge(scattered, i * 16 + 16)
                nc.scalar.activation(ysb[:, 0:512], pv_bank[0][0:BLK, :], ACT.Copy, scale=gate_now[:, 0:1]
                                     ).then_inc(y0_ready, 1)

            nc.scalar.preload_act_table_set("natural_log_exp_and_others")
            act.dma_start(fing, final_norm_g.rearrange("(a d) -> a d", a=1).to_broadcast([P, D])).then_inc(fing_in, 16)
            act.wait_ge(scattered, n_items * 16 + 16)
            for t in range(NT):
                act.dma_start(xres[:, t, :], acc_rows[t * P:(t + 1) * P, :]).then_inc(x_in[t], 16)
            for t in range(NT):
                act.wait_ge(x_in[t], 32)
                nc.scalar.activation(rows[:, t, :], xres[:, t, :], ACT.Square, accum_out=ssq[:, t:t + 1]).then_inc(ssf, 1)
                root(t, 1)

        @block.vector
        def _(dve):
            chain = [0]

            def link(ins):
                chain[0] += 1
                ins.then_inc(dstep, 1)
                dve.wait_ge(dstep, chain[0])

            rms_count = [0]

            def rms(col, n, width, src=None):
                c = slice(col, col + n)
                nc.vector.tensor_scalar(msq[:, c], ssq[:, c] if src is None else src, 1.0 / width, EPS, ALU.mult, ALU.add).then_inc(msq_ready, 1)
                rms_count[0] += 1
                dve.wait_ge(root_ready, rms_count[0])
                link(nc.vector.reciprocal(rstd[:, c], rstd[:, c]))

            for t in range(NT):
                dve.wait_ge(ssx, t + 1)
                rms(t, 1, D)
                nc.vector.tensor_scalar(rows[:, t, :], xres[:, t, :], rstd[:, t:t + 1], None, ALU.mult
                                        ).then_inc(xn_ready, 1)
            dve.wait_ge(g_in, 64)
            for k in range(1, KD, 2):
                dve.wait_ge(tr_done, k + 1)
                nc.vector.tensor_scalar(colsT[:, k, :], pj_bank[1][:, :], g_attn[:, k:k + 1], None, ALU.mult
                                        ).then_inc(tr_used_v, 1)
            def read_bgu():
                dve.wait_ge(bgu_done, 1)
                nc.vector.tensor_copy(bgu[:].rearrange("p e c -> p c e"),
                                      pt_bank[0][:, :].rearrange("p (c e) -> p c e", e=NE)).then_inc(bgu_read, 1)

            def forget_z():
                dve.wait_ge(f_in, 32)
                dve.wait_ge(f_done, 1)
                nc.vector.tensor_scalar(zf, pt_bank[1][0:HEADS, :], bf_c[:, 0:1], -1.0, ALU.add, ALU.mult
                                        ).then_inc(zf_ready, 1)

            def forget_sum():
                dve.wait_ge(lf_abs, 1)
                link(nc.vector.scalar_tensor_tensor(out=lf, in0=zf, scalar=0.0, in1=lf, op0=ALU.max, op1=ALU.add))
                dve.wait_ge(consts, 13)
                nc.vector.tensor_tensor_scan(out=negc_sb, data0=onesrow[0:HEADS, 0:1].to_broadcast([HEADS, SEQ]),
                                             data1=lf, initial=0.0, op0=ALU.mult, op1=ALU.add).then_inc(negc_ready, 1)

            def arg(u):
                g, h, t = tile_of(u)
                w = (t + 1) * P
                if g == 0:
                    dve.wait_ge(softln, u + 1)
                    z = sc_bank[u % 2][:, 0:w]
                    link(nc.vector.scalar_tensor_tensor(out=wk[:, 2, 0:w], in0=z, scalar=0.0, in1=wk[:, u % 2, 0:w],
                                                        op0=ALU.max, op1=ALU.add))
                    link(nc.vector.tensor_tensor_scan(out=wk[:, 3, w - 1::-1], data0=onesrow[:, 0:1].to_broadcast([P, w]),
                                                      data1=wk[:, 2, w - 1::-1], initial=0.0,
                                                      op0=ALU.mult, op1=ALU.add))
                    if u >= 2:
                        dve.wait_ge(probT_done, u - 1)
                    nc.vector.tensor_tensor(wk[:, 4 + u % 2, 0:w], z, wk[:, 3, 0:w], ALU.subtract).then_inc(arg_ready, 1)
                else:
                    c = u - 32
                    dve.wait_ge(score_done, u + 1)
                    if c == 0:
                        dve.wait_ge(negc_in, 16)
                    if c >= 4:
                        dve.wait_ge(probT_done, u - 3)
                    nc.vector.tensor_tensor_reduce(out=prob_tile(u)[:, 0:w], in0=sc_bank[u % 2][:, 0:w],
                                                   in1=negc[:, h, 0:w], scale=-1.0, scalar=3e38, op0=ALU.add,
                                                   op1=ALU.min, accum_out=nmax[:, c:c + 1]).then_inc(arg_ready, 1)

            def copy_probT(u):
                g, h, t = tile_of(u)
                w = (t + 1) * P
                dve.wait_ge(probT_done, u + 1)
                if u >= 2:
                    dve.wait_ge(pv_done, u // 2)
                nc.vector.tensor_copy(wk[:, 6 + u % 2, 0:w], pt_bank[u % 2][:, 0:w]).then_inc(probT_v, 1)

            def scale_prob(u):
                g, h, t = tile_of(u)
                c, w = u - 32, (t + 1) * P
                dve.wait_ge(prob_ready, u + 1)
                link(nc.vector.reciprocal(rinv[:, c:c + 1], rsum[:, c:c + 1]))
                nc.vector.tensor_scalar(prob_tile(u)[:, 0:w], prob_tile(u)[:, 0:w], rinv[:, c:c + 1], None, ALU.mult
                                        ).then_inc(scaled, 1)

            def read_y(c):
                dve.wait_ge(sq_ready, c + 1)
                k = (4 if c < 4 else 0) + c % 4
                nc.vector.tensor_scalar(yT[:, k, :], pv_bank[c % 2][:, :], g_mix[:, k:k + 1], None, ALU.mult
                                        ).then_inc(y_ready, 1)

            def norm_y(g):
                dve.wait_ge(ssy_done, g + 1)
                rms(4 + 4 * g, 4, GW, ssq_bank[g][:, 0:8].rearrange("p (t a) -> p t a", a=2)[:, :, 0])

            def read_op(m):
                g, t, half = m // 8, (m % 8) // 2, m % 2
                dve.wait_ge(op_done, m + 1)
                c = slice(half * 512, half * 512 + 512)
                nc.vector.scalar_tensor_tensor(out=xres[:, t, c], in0=pj_bank[m % 2][:, :],
                                               scalar=rstd[:, 4 + 4 * g + t:5 + 4 * g + t], in1=xres[:, t, c],
                                               op0=ALU.mult, op1=ALU.add).then_inc(x1_ready, 1)

            dve.wait_ge(tr_done, KD)
            for n in range(NU // 2 + 3):
                if n == 0:
                    read_bgu()
                    forget_z()
                for u in (2 * n - 2, 2 * n - 1):
                    if 32 <= u < NU:
                        scale_prob(u)
                for u in (2 * n, 2 * n + 1):
                    if u < NU:
                        arg(u)
                if n == 0:
                    forget_sum()
                for u in (2 * n - 2, 2 * n - 1):
                    if 0 <= u < 32:
                        copy_probT(u)
                if n >= 6 and (n - 6) % 4 == 0:
                    read_y((n - 6) // 4)
                if n == 20:
                    norm_y(0)
                if n - 1 in OUT_B_STEPS:
                    read_op(OUT_B_STEPS.index(n - 1))
            norm_y(1)

            def norm_1(t):
                dve.wait_ge(ss1, t + 1)
                rms(12 + t, 1, D)
                nc.vector.tensor_scalar(h2[:, t, :], xres[:, t, :], rstd[:, 12 + t:13 + t], None, ALU.mult
                                        ).then_inc(h2_ready, 1)

            def read_h2t(t):
                for hf in range(2):
                    dve.wait_ge(h2t_done, 2 * t + hf + 1)
                    nc.vector.tensor_tensor(h2T[:, 4 * hf:4 * hf + 4, t * P:(t + 1) * P],
                                            pt_bank[hf][:, :].rearrange("p (k c) -> p k c", c=P),
                                            g_ffn[:, 4 * hf:4 * hf + 4].rearrange("p (k a) -> p k a", a=1)
                                            .to_broadcast([P, 4, P]), ALU.mult).then_inc(h2t_read, 1)

            def route(ts):
                a, b = ts[0], ts[-1] + 1
                n = b - a
                dve.wait_ge(r_in, 32)
                for t in ts:
                    dve.wait_ge(rt_done, t + 1)
                    nc.vector.scalar_tensor_tensor(out=logits[:, t, :], in0=logit_bank[t][:, 0:NE],
                                                   scalar=rstd[:, 12 + t:13 + t], in1=br_b[:], op0=ALU.mult, op1=ALU.add
                                                   ).then_inc(rt_read, 1)
                for t in ts:
                    dve.wait_ge(rt_read, t + 1)
                    ins = nc.vector.max(top8[:, t, :], logits[:, t, :])
                link(ins)
                for t in ts:
                    ins = nc.vector.max_index(topi[:, t, :], top8[:, t, :], logits[:, t, :])
                link(ins)
                for t in ts:
                    nc.vector.tensor_scalar(gexp[:, t, :], top8[:, t, 0:TOPK], top8[:, t, 0:1], None, ALU.subtract
                                            ).then_inc(gl_ready, 1)
                link(nc.vector.tensor_copy(topk_places[:, a * TOPK:b * TOPK].rearrange("p (t k) -> p t k", k=TOPK),
                                           topi[:, a:b, 0:TOPK]))
                oh = onehot[:, a:b].rearrange("p t k e -> p (t k) e")
                link(nc.vector.tensor_tensor(
                    oh, iota[:, 0:NE].rearrange("p (b e) -> p b e", b=1).to_broadcast([P, n * TOPK, NE]),
                    topk_places[:, a * TOPK:b * TOPK].rearrange("p (k a) -> p k a", a=1).to_broadcast([P, n * TOPK, NE]),
                    ALU.is_equal))
                link(nc.vector.tensor_reduce(maskf[:, a:b, :], onehot[:, a:b].rearrange("p t k e -> p t e k"), AX.X,
                                             ALU.add))
                nc.vector.tensor_copy(maskb[:, a:b, :], maskf[:, a:b, :]).then_inc(mask_ready, n)

            def gates():
                dve.wait_ge(y0_ready, NT)
                link(nc.vector.tensor_reduce(gsum[:], gexp[:], AX.X, ALU.add))
                link(nc.vector.reciprocal(ginv[:], gsum[:]))
                link(nc.vector.tensor_tensor(gexp[:], gexp[:],
                                             ginv[:].rearrange("p (t a) -> p t a", a=1).to_broadcast([P, NT, TOPK]),
                                             ALU.mult))
                link(nc.vector.tensor_tensor(onehot_g.rearrange("p t k e -> p (t k) e"),
                                             onehot.rearrange("p t k e -> p (t k) e"),
                                             gexp[:].rearrange("p t (k a) -> p (t k) a", a=1)
                                             .to_broadcast([P, NT * TOPK, NE]), ALU.mult))
                link(nc.vector.tensor_reduce(gate_et[:].rearrange("p (e t) -> p t e", t=NT),
                                             onehot_g.rearrange("p t k e -> p t e k"), AX.X, ALU.add))

            for t in range(NT):
                read_op(8 + 2 * t)
                read_op(9 + 2 * t)
                if t >= 1:
                    read_h2t(t - 1)
                norm_1(t)
            read_h2t(NT - 1)
            route((0, 1))
            route((2, 3))
            dve.wait_ge(rank_done, 1)
            link(nc.vector.scalar_tensor_tensor(
                out=rank_et[:].rearrange("p (e t) -> p t e", t=NT), in0=maskf, scalar=-FAR,
                in1=pj_bank[0][:, 0:NT * NE].rearrange("p (t e) -> p t e", e=NE), op0=ALU.mult, op1=ALU.add))
            link(nc.vector.tensor_copy(counts[:], pj_bank[0][:, NT * NE:(NT + 1) * NE]))
            link(nc.vector.tensor_scalar(rel[:], rank_et[:, 0:NT], item_b[:, 0:1], None, ALU.subtract))
            for t in range(NT):
                ins = nc.vector.tensor_scalar(sel[:, t, :], iota[:, 0:BLK], rel[:, t:t + 1], None, ALU.is_equal)
            ins.then_inc(sel_ready, 1)

            def read_idx(idx_next):
                ps = pj_bank[0]
                nc.vector.tensor_reduce(idsum[:], ps[0:BLK, 0:2], AX.X, ALU.add)
                link(nc.vector.tensor_scalar(padsel[:], ps[0:BLK, 2:3], 0.0, padrow[0:BLK, 0:1], ALU.is_equal, ALU.mult))
                nc.vector.tensor_tensor(idx_next[:], padsel[:], idsum[:], ALU.add).then_inc(idx_ready, 1)

            def read_xt():
                for hf in range(2):
                    ins = nc.vector.tensor_tensor(
                        xgT[:, 4 * hf:4 * hf + 4, :], pt_bank[hf][:, 0:4 * BLK].rearrange("p (k c) -> p k c", c=BLK),
                        g_ffn[:, 4 * hf:4 * hf + 4].rearrange("p (k a) -> p k a", a=1).to_broadcast([P, 4, BLK]),
                        ALU.mult)
                ins.then_inc(xt_ready, 1)

            dve.wait_ge(idx_done, 1)
            read_idx(idx_mid)
            gates()
            link(nc.vector.tensor_copy(gate3[:, :, 0], gate_et[:]))
            link(nc.vector.tensor_tensor(gate_rest, gate_et[:], gate3[:, :, 0], ALU.subtract))
            link(nc.vector.tensor_copy(gate3[:, :, 1], gate_rest))
            link(nc.vector.tensor_tensor(gate_rest, gate_rest, gate3[:, :, 1], ALU.subtract))
            link(nc.vector.tensor_copy(gate3[:, :, 2], gate_rest))
            nc.vector.tensor_copy(info[:, :, 3:6], gate3[:, 0:NT, :]).then_inc(gu_used, 2)
            dve.wait_ge(idx_done, 2)
            nc.vector.tensor_reduce(gate_mid[:], pj_bank[0][0:BLK, 3:6], AX.X, ALU.add)
            link(nc.vector.tensor_scalar(rel[:], rank_et[:, NT:2 * NT], item_b[:, 1:2], None, ALU.subtract))
            nc.vector.tensor_copy(info[:, :, 3:6], gate3[:, NT:2 * NT, :])
            for t in range(NT):
                ins = nc.vector.tensor_scalar(sel[:, t, :], iota[:, 0:BLK], rel[:, t:t + 1], None, ALU.is_equal)
            ins.then_inc(sel_ready, 1)
            nc.vector.tensor_scalar(item_few[:, 0:NE], counts[0:1, :], float(FEW), None, ALU.is_le)
            link(nc.vector.tensor_scalar(few_sum[:], counts[0:1, :], float(FEW), None, ALU.is_le))
            link(nc.vector.tensor_tensor_scan(out=few_sum[:], data0=onesrow[0:1, :], data1=few_sum[:], initial=0.0,
                                              op0=ALU.mult, op1=ALU.add))
            nc.vector.tensor_copy(few_before[:, 1:NE], few_sum[:, 0:NE - 1])
            link(nc.vector.tensor_scalar(extra[:], counts[:], float(BLK), None, ALU.is_gt))
            for b in range(2, MAXBLK):
                link(nc.vector.scalar_tensor_tensor(out=extra[:], in0=counts[:], scalar=float(b * BLK), in1=extra[:],
                                                    op0=ALU.is_gt, op1=ALU.add))
            link(nc.vector.tensor_tensor_scan(out=cumx[:], data0=onesrow[:], data1=extra[:], initial=0.0,
                                              op0=ALU.mult, op1=ALU.add))
            nc.vector.tensor_scalar(n_items_sb[:, 1:2], cumx[0:1, NE - 1:NE], float(NE - 1), None, ALU.add)
            link(nc.vector.tensor_scalar(n_items_sb[:, 0:1], cumx[0:1, NE - 1:NE], float(NE), None, ALU.add))
            nc.vector.memset(biasc[:], 0.0).then_inc(count_ready, 1)
            dve.wait_ge(idx_done, 3)
            nc.vector.tensor_reduce(gate_next[:], pj_bank[0][0:BLK, 3:6], AX.X, ALU.add)
            read_idx(idx_next)
            dve.wait_ge(xt_done, 1)
            read_xt()
            cum_b = cumx[:].rearrange("p (a e) -> p a e", a=1).to_broadcast([P, NX, NE])
            ext_b = extra[:].rearrange("p (a e) -> p a e", a=1).to_broadcast([P, NX, NE])
            j_b = iota[:, 0:NX].rearrange("p (j a) -> p j a", a=1).to_broadcast([P, NX, NE])
            link(nc.vector.tensor_tensor(itemcmp, cum_b, j_b, ALU.is_le))
            link(nc.vector.tensor_tensor(itemcmp2, itemcmp, ext_b, ALU.mult))
            link(nc.vector.tensor_reduce(item_f[:, NE:NI], itemcmp, AX.X, ALU.add))
            link(nc.vector.tensor_scalar(item_f[:, NE:NI], item_f[:, NE:NI], float(NE - 1), None, ALU.min))
            link(nc.vector.tensor_reduce(cxj[:], itemcmp2, AX.X, ALU.add))
            link(nc.vector.tensor_tensor(cxj[:], iota[:, 0:NX], cxj[:], ALU.subtract))
            link(nc.vector.tensor_scalar(item_b[:, NE:NI], cxj[:], float(BLK), float(BLK) - FAR, ALU.mult, ALU.add))
            nc.vector.tensor_copy(item_e[:], item_f[0:1, :]).then_inc(items_ready, 1)
            dve.wait_ge(items_ready, 1)

            nc.vector.memset(biasc[:], 0.0).then_inc(y1_ready, 1)
            dve.wait_ge(y1_ready, 1)

            dve.wait_ge(bdown_ready, 1)
            n_items = dve.value_load(n_items_sb[0:1, 0:1], min_val=NE, max_val=NE + EXTRA_MAX)
            with dve.Fori(0, n_items) as i:
                e_now = dve.value_load(item_e[0:1, bass.ds(i, 1)], min_val=0, max_val=NE - 1)
                e_next = dve.value_load(item_e[0:1, bass.ds(i + 2, 1)], min_val=0, max_val=NE - 1)
                nc.vector.tensor_copy(biasc[:], bgu[:].rearrange("p e c -> p (e c)")[:, bass.ds(e_now * 16, 16)]
                                      ).then_inc(bias_ready, 1)
                nc.vector.tensor_copy(esel, ident3[:, bass.ds(e_now, 1)].to_broadcast([3 * NE, BLK])).then_inc(esel_ready, 1)
                dve.wait_ge(idx_done, i + 3)
                nc.vector.tensor_scalar(rel[:], rank_et[:, bass.ds(e_next * NT, NT)], item_b[:, bass.ds(i + 2, 1)],
                                        None, ALU.subtract).then_inc(rel_ready, 1)
                nc.vector.tensor_copy(info[:, :, 3:6], gate3[:, bass.ds(e_next * NT, NT), :])
                dve.wait_ge(rel_ready, i + 1)
                for t in range(NT):
                    ins = nc.vector.tensor_scalar(sel[:, t, :], iota[:, 0:BLK], rel[:, t:t + 1], None, ALU.is_equal)
                ins.then_inc(sel_ready, 1)
                dve.wait_ge(bias_ready, i + 1)
                for q in range(4):
                    gt, ut, st, ps = gtile[q % 2], utile[q % 2], stile[q % 2], sc_bank[q % 2]
                    dve.wait_ge(gu_done, i * 4 + (q + 1))
                    for jj in range(2):
                        c = 4 * q + 2 * jj
                        gi = nc.vector.tensor_scalar(gt[:, jj, :], ps[:, (2 * jj) * BLK:(2 * jj + 1) * BLK],
                                                     biasc[:, c:c + 1], LIMIT, ALU.add, ALU.min)
                    gi.then_inc(g_ready, 1)
                    for jj in range(2):
                        c = 4 * q + 2 * jj + 1
                        ui = nc.vector.tensor_scalar(ut[:, jj, :], ps[:, (2 * jj + 1) * BLK:(2 * jj + 2) * BLK],
                                                     biasc[:, c:c + 1], LIMIT, ALU.add, ALU.min)
                    ui.then_inc(gu_used, 1)
                    dve.wait_ge(gu_used, i * 4 + (q + 3))
                    nc.vector.tensor_scalar(ut, ut, -LIMIT, 1.0, ALU.max, ALU.add).then_inc(u_step, 1)
                    dve.wait_ge(u_step, i * 8 + (2 * q + 1))
                    dve.wait_ge(g_ready, i * 4 + (q + 1))
                    nc.vector.tensor_tensor(ut, gt, ut, ALU.mult).then_inc(u_step, 1)
                    dve.wait_ge(u_step, i * 8 + (2 * q + 2))
                    dve.wait_ge(s_ready, i * 4 + (q + 1))
                    nc.vector.tensor_tensor(actT[:, 2 * q:2 * q + 2, :], ut, st, ALU.mult).then_inc(act_ready, 1)
                dve.wait_ge(xt_done, i + 2)
                read_xt()
                dve.wait_ge(scattered, i * 16 + 16)
                nc.vector.tensor_copy(gate_now[:], gate_mid[:])
                nc.vector.tensor_copy(idx_now[:], idx_mid[:]).then_inc(now_ready, 1)
                dve.wait_ge(now_ready, i * 2 + 1)
                nc.vector.tensor_copy(gate_mid[:], gate_next[:])
                nc.vector.tensor_copy(idx_mid[:], idx_next[:]).then_inc(now_ready, 1)
                dve.wait_ge(now_ready, i * 2 + 2)
                dve.wait_ge(idx_done, i + 4)
                ps0 = pj_bank[0]
                nc.vector.tensor_reduce(gate_next[:], ps0[0:BLK, 3:6], AX.X, ALU.add)
                nc.vector.tensor_reduce(idsum[:], ps0[0:BLK, 0:2], AX.X, ALU.add)
                nc.vector.tensor_scalar(padsel[:], ps0[0:BLK, 2:3], 0.0, padrow[0:BLK, 0:1], ALU.is_equal,
                                        ALU.mult).then_inc(pad_step, 1)
                dve.wait_ge(pad_step, i + 1)
                nc.vector.tensor_tensor(idx_next[:], padsel[:], idsum[:], ALU.add).then_inc(idx_ready, 1)
                dve.wait_ge(down_done, i + 1)
                few = dve.value_load(item_few[0:1, bass.ds(i, 1)], min_val=0, max_val=1)
                with dve.If(few):
                    nc.vector.tensor_scalar(ysb[0:FEW, 512:D], pv_bank[1][FEW:2 * FEW, :], gate_now[0:FEW, 0:1], None,
                                            ALU.mult).then_inc(y1_ready, 1)
                with dve.Else():
                    nc.vector.tensor_scalar(ysb[:, 512:D], pv_bank[1][0:BLK, :], gate_now[:, 0:1], None, ALU.mult
                                            ).then_inc(y1_ready, 1)

            for t in range(NT):
                dve.wait_ge(ssf, t + 1)
                rms(t, 1, D)
                dve.wait_ge(fing_in, 16)
                nc.vector.scalar_tensor_tensor(out=rows[:, t, :], in0=xres[:, t, :], scalar=rstd[:, t:t + 1], in1=fing,
                                               op0=ALU.mult, op1=ALU.mult).then_inc(fin_ready, 1)

        @block.tensor
        def _(pe):
            pe.wait_ge(consts, 1)
            pe.wait_ge(xn_ready, NT)
            for k in range(KD):
                if k >= 2:
                    pe.wait_ge(tr_used_a if k % 2 == 0 else tr_used_v, k // 2)
                for t in range(NT):
                    last = nc.tensor.transpose(pj_bank[k % 2][:, t * P:(t + 1) * P], rows[:, t, k * P:(k + 1) * P],
                                               ident[:])
                last.then_inc(tr_done, 1)
            pe.wait_ge(tr_used_a, KD // 2)
            pe.wait_ge(tr_used_v, KD // 2)
            def transpose_bgu():
                pe.wait_ge(bgu_in, 16)
                for c in range(16):
                    q, r = c // 2, c % 2
                    last = nc.tensor.transpose(pt_bank[0][:, c * NE:(c + 1) * NE],
                                               bgu_rows[:, q * 256 + r:q * 256 + r + 255:2], ident[0:NE, 0:NE])
                last.then_inc(bgu_done, 1)

            def forget_logits():
                pe.wait_ge(f_in, 32)
                for k in range(KD):
                    last = nc.tensor.matmul(pt_bank[1][0:HEADS, :], w_f[:, k, :], colsT[:, k, :],
                                            start=(k == 0), stop=(k == KD - 1))
                last.then_inc(f_done, 1)

            def project(n):
                g, c = n // 4, n % 4
                w = mix_tile(g)
                if c == 0:
                    pe.wait_ge(landed[g % MIX_SLOTS], 16 * (g // MIX_SLOTS + 1))
                if n >= 2:
                    pe.wait_ge(proj_read, n - 1)
                ps = pj_bank[n % 2]
                for k in range(KD):
                    if g in (2, 5):
                        last = nc.tensor.matmul(ps[:, :], colsT[:, k, c * P:(c + 1) * P], w[:, k, :],
                                                start=(k == 0), stop=(k == KD - 1))
                    else:
                        last = nc.tensor.matmul(ps[:, :], w[:, k, c * P:(c + 1) * P], colsT[:, k, :],
                                                start=(k == 0), stop=(k == KD - 1))
                last.then_inc(proj_done, 1)

            def scores(n):
                g, _, t = tile_of(2 * n)
                if n == 0:
                    pe.wait_ge(proj_read, 8)
                    pe.wait_ge(consts, 13)
                if n == 16:
                    pe.wait_ge(proj_read, 20)
                if n >= 1:
                    pe.wait_ge(arg_ready, 2 * n)
                for lo, hi in ((0, t * P), (t * P, (t + 1) * P)):
                    if lo == hi:
                        continue
                    for j in (0, 1):
                        h = tile_of(2 * n + j)[1]
                        c, r = (0 if g == 0 else 8) + h // 2, slice(j * DH, (j + 1) * DH)
                        nc.tensor.matmul(sc_bank[j][:, lo:hi], qk[r, c, t * P:(t + 1) * P], qk[r, c + 4, lo:hi],
                                         start=True, stop=(lo < t * P))
                for j in (0, 1):
                    nc.tensor.matmul(sc_bank[j][:, t * P:(t + 1) * P], identb[:],
                                     (mask_strict if g == 0 else mask_causal)[:], start=False, stop=True
                                     ).then_inc(score_done, 1)

            def transpose_prob(u):
                g, h, t = tile_of(u)
                if g == 0:
                    pe.wait_ge(prob_ready, u + 1)
                else:
                    pe.wait_ge(scaled, u - 31)
                if u >= 2:
                    if u - 2 < 32:
                        pe.wait_ge(probT_v, u - 1)
                    else:
                        pe.wait_ge(probT_a, u - 33)
                for s in range(t + 1):
                    last = nc.tensor.transpose(pt_bank[u % 2][:, s * P:(s + 1) * P],
                                               prob_tile(u)[:, s * P:(s + 1) * P], ident[:])
                last.then_inc(probT_done, 1)

            def attend(n):
                g, _, t = tile_of(2 * n)
                c = n // NT
                if g == 0:
                    pe.wait_ge(probT_v, 2 * n + 2)
                else:
                    pe.wait_ge(probT_a, 2 * n - 30)
                if t == 0 and c >= 2:
                    pe.wait_ge(y_ready, c - 1)
                pe.wait_ge(proj_read, 8 + t + 1 if g == 0 else 20 + t + 1)
                for s in range(t + 1):
                    for j in (0, 1):
                        o = (GW if g == 0 else 0) + tile_of(2 * n + j)[1] * DH
                        last = nc.tensor.matmul(pv_bank[c % 2][j * DH:(j + 1) * DH, t * P:(t + 1) * P],
                                                v_sb[:, s, o:o + DH], wk[:, 6 + j, s * P:(s + 1) * P],
                                                start=(s == 0), stop=(s == t))
                last.then_inc(pv_done, 1)

            def sum_squares(g):
                pe.wait_ge(sq_summed, 4 * (g + 1))
                for t in range(NT):
                    last = nc.tensor.matmul(ssq_bank[g][:, 2 * t:2 * t + 2], sqsum[:, t * P:(t + 1) * P], onescol[:],
                                            start=True, stop=True)
                last.then_inc(ssy_done, 1)

            def project_out(m):
                g, t, half = m // 8, (m % 8) // 2, m % 2
                if m % 8 == 0:
                    n = 6 + g
                    pe.wait_ge(landed[n % MIX_SLOTS], 16 * (n // MIX_SLOTS + 1))
                    pe.wait_ge(y_ready, 4 * (g + 1))
                    if g == 0:
                        pe.wait_ge(msq_ready, 5)
                if m >= 2:
                    pe.wait_ge(x1_ready, m - 1)
                w = mix_tile(6 + g)
                for k in range(4):
                    last = nc.tensor.matmul(pj_bank[m % 2][:, :], yT[:, (4 if g == 0 else 0) + k, t * P:(t + 1) * P],
                                            w[:, k, half * 512:half * 512 + 512], start=(k == 0), stop=(k == 3))
                last.then_inc(op_done, 1)

            for n in range(8):
                project(n)
            transpose_bgu()
            forget_logits()
            for n in range(NU // 2 + 3):
                if n < 16:
                    project(8 + n)
                if n < NU // 2:
                    scores(n)
                if 0 <= n - 2 < NU // 2:
                    attend(n - 2)
                for u in (2 * n - 2, 2 * n - 1):
                    if 0 <= u < NU:
                        if u == 0:
                            pe.wait_ge(bgu_read, 1)
                            pe.wait_ge(zf_ready, 1)
                        transpose_prob(u)
                if n == 19:
                    sum_squares(0)
                if n in OUT_B_STEPS:
                    project_out(OUT_B_STEPS.index(n))

            def transpose_h2(t):
                pe.wait_ge(x1_ready, 8 + 2 * (t + 1))
                for hf in range(2):
                    if t >= 1:
                        pe.wait_ge(h2t_read, 2 * t - 1 + hf)
                    for k in range(4):
                        kk = 4 * hf + k
                        last = nc.tensor.transpose(pt_bank[hf][:, k * P:(k + 1) * P], xres[:, t, kk * P:(kk + 1) * P],
                                                   ident[:])
                    last.then_inc(h2t_done, 1)

            def router(t):
                pe.wait_ge(h2t_read, 2 * t + 2)
                pe.wait_ge(r_in, 32)
                for k in range(KD):
                    last = nc.tensor.matmul(logit_bank[t][:, 0:NE], h2T[:, k, t * P:(t + 1) * P], w_r[:, k, :],
                                            start=(k == 0), stop=(k == KD - 1))
                last.then_inc(rt_done, 1)

            for t in range(NT):
                project_out(8 + 2 * t)
                project_out(9 + 2 * t)
                if t == 0:
                    sum_squares(1)
                if t > 0:
                    transpose_h2(t - 1)
                if t > 1:
                    router(t - 2)
            transpose_h2(NT - 1)
            router(NT - 2)
            router(NT - 1)

            pe.wait_ge(mask_ready, NT)
            pe.wait_ge(x1_ready, 4 * NT)
            for t in range(NT + 1):
                top = min(t, NT - 1)
                for s in range(top + 1):
                    last = nc.tensor.matmul(pj_bank[0][:, t * NE:(t + 1) * NE], (before if s == t else ones)[:],
                                            maskb[:, s, :], start=(s == 0), stop=(s == top))
            last.then_inc(rank_done, 1)
            def slot_rows():
                for t in range(NT):
                    last = nc.tensor.matmul(pj_bank[0][0:BLK, 0:6], sel[:, t, :], info[:, t, :],
                                            start=(t == 0), stop=(t == NT - 1))
                last.then_inc(idx_done, 1)

            def transpose_x():
                for k in range(KD):
                    hf, kk = k // 4, k % 4
                    last = nc.tensor.transpose(pt_bank[hf][:, kk * BLK:(kk + 1) * BLK], xg[:, k * P:(k + 1) * P],
                                               ident[0:BLK, 0:BLK])
                last.then_inc(xt_done, 1)

            pe.wait_ge(sel_ready, 1)
            slot_rows()
            pe.wait_ge(gu_used, 2)
            pe.wait_ge(idx_ready, 1)
            slot_rows()
            pe.wait_ge(gathered, 16)
            transpose_x()
            pe.wait_ge(sel_ready, 2)
            slot_rows()
            pe.wait_ge(count_ready, 1)
            pe.wait_ge(bdown_ready, 1)
            pe.wait_ge(half_ready, 1)

            n_items = pe.value_load(n_items_sb[0:1, 0:1], min_val=NE, max_val=NE + EXTRA_MAX)
            with pe.Fori(0, n_items) as i:
                pe.wait_ge(xt_ready, i + 1)
                few = pe.value_load(item_few[0:1, bass.ds(i, 1)], min_val=0, max_val=1)
                odd = pe.value_load(item_odd[0:1, bass.ds(i, 1)], min_val=0, max_val=1)
                half_i = pe.value_load(item_half[0:1, bass.ds(i, 1)], min_val=0, max_val=NI // 2)
                before_i = pe.value_load(few_before[0:1, bass.ds(i, 1)], min_val=0, max_val=NE)

                def next_slots():
                    pe.wait_ge(sel_ready, i + 3)
                    slot_rows()

                def await_piece(q, is_odd):
                    if q >= TWICE:
                        pe.wait_ge(landed[q], i * 16 + (48 if q < MIX_SLOTS else 16))
                    elif is_odd:
                        pe.wait_ge(landed_odd[q], half_i * 16 + 16)
                    else:
                        pe.wait_ge(landed[q], half_i * 16 + 48)

                def gate_up(q, is_odd):
                    await_piece(q, is_odd)
                    pe.wait_ge(gu_used, i * 4 + (q + 1))
                    w = gu_tile(q, is_odd)
                    for jj in range(2):
                        for r in range(2):
                            o = (2 * jj + r) * BLK
                            for k in range(KD):
                                last = nc.tensor.matmul(sc_bank[q % 2][:, o:o + BLK],
                                                        w[:, k, jj * 256 + r:jj * 256 + r + 255:2], xgT[:, k, :],
                                                        start=(k == 0), stop=(k == KD - 1))
                    last.then_inc(gu_done, 1)

                def gate_up_rows(p, ks, is_odd):
                    for k in ks:
                        for h in range(2):
                            if k == 0:
                                await_piece(2 * p + h, is_odd)
                            last = nc.tensor.matmul(pt_bank[p][h * FEW:(h + 1) * FEW, :], xgT[:, k, 0:FEW],
                                                    gu_tile(2 * p + h, is_odd)[:, k, :], start=(k == 0), stop=(k == KD - 1))
                    if ks[-1] == KD - 1:
                        last.then_inc(rows_done, 1)

                def await_rows(p):
                    pe.wait_ge(rows_read, before_i * 2 + (p + 1))
                    pe.wait_ge(gu_used, i * 4 + (2 * p + 2))

                def turn_rows(p):
                    for h in range(2):
                        for jj in range(2):
                            for r in range(2):
                                o = (2 * jj + r) * BLK
                                hs = slice(h * FEW, (h + 1) * FEW)
                                last = nc.tensor.transpose(sc_bank[h][:, o:o + FEW],
                                                           gu_rows[hs, p, jj * 256 + r:jj * 256 + r + 255:2],
                                                           ident[hs, hs])
                        last.then_inc(gu_done, 1)

                def down_bias(rows, first):
                    pe.wait_ge(y0_ready, i + NT)
                    pe.wait_ge(y1_ready, i + 1)
                    pe.wait_ge(esel_ready, i + 1)
                    for half in range(2):
                        nc.tensor.matmul(pv_bank[half][first[half]:first[half] + rows, :], esel[:, 0:rows],
                                         bdown3[:, half * 512:half * 512 + 512], start=True, stop=False)

                def down(rows, first, ks):
                    for k in ks:
                        if k % 4 == 0:
                            await_piece(4 + k // 4, False)
                        if k % 2 == 0:
                            pe.wait_ge(act_ready, i * 4 + (k // 2 + 1))
                        if k == 4:
                            pe.wait_ge(gathered, i * 16 + 32)
                            transpose_x()
                        w = down_tile(k // 4)
                        for half in range(2):
                            last = nc.tensor.matmul(pv_bank[half][first[half]:first[half] + rows, :], actT[:, k, 0:rows],
                                                    w[:, k % 4, half * 512:half * 512 + 512],
                                                    start=False, stop=(k == KD - 1))
                        if k == 3:
                            last.then_inc(half_done, 1)
                    if ks[-1] == KD - 1:
                        last.then_inc(down_done, 1)

                def few_tokens(is_odd):
                    gate_up_rows(0, range(KD), is_odd)
                    next_slots()
                    gate_up_rows(1, range(0, 1), is_odd)
                    await_rows(0)
                    gate_up_rows(1, range(1, 2), is_odd)
                    turn_rows(0)
                    gate_up_rows(1, range(2, KD), is_odd)
                    down_bias(FEW, (0, FEW))
                    down(FEW, (0, FEW), range(0, 1))
                    await_rows(1)
                    down(FEW, (0, FEW), range(1, 2))
                    turn_rows(1)
                    down(FEW, (0, FEW), range(2, KD))

                def many_tokens(is_odd):
                    gate_up(0, is_odd)
                    next_slots()
                    for q in range(1, 4):
                        gate_up(q, is_odd)
                    down_bias(BLK, (0, 0))
                    down(BLK, (0, 0), range(KD))

                with pe.If(few):
                    with pe.If(odd):
                        few_tokens(True)
                    with pe.Else():
                        few_tokens(False)
                with pe.Else():
                    with pe.If(odd):
                        many_tokens(True)
                    with pe.Else():
                        many_tokens(False)


_INS = ["x", "attn_norm_g", "w_in", "b_forget", "fox_out_g", "sb_out_g", "w_out", "ffn_norm_g", "w_router", "b_router",
        "w_gate_up", "b_gate_up", "w_down", "b_down", "final_norm_g"]


def kernel(**inputs):
    import numpy as _np
    import concourse.bacc as _bacc
    from concourse import mybir as _mybir
    from concourse.bass_utils import run_bass_kernel_spmd as _run

    nc = _bacc.Bacc("TRN2", target_bir_lowering=False, num_devices=1)
    arrays, args = {}, []
    for name in _INS:
        a = _np.ascontiguousarray(inputs[name])
        arrays[f"in_{name}_dram"] = a
        args.append(nc.dram_tensor(f"in_{name}_dram", a.shape, _mybir.dt.from_np(a.dtype), kind="ExternalInput").ap())
    args.append(nc.dram_tensor("out_0_dram", (1, SEQ, D), _mybir.dt.float32, kind="ExternalOutput").ap())
    hybrid_layer(nc, *args)
    r = _run(nc, [arrays], core_ids=[0])
    return r.results[0]["out_0_dram"]
```
